# Optimizing a Trainium2 kernel written in Bass

```python
import jax, jax.numpy as jnp
from jax import lax
import numpy as np

D_MODEL = 1024
BATCH = 1
SEQ = 128
DEPTH = 2
DEC_BATCH = 1
DEC_SEQ = 512
PAST_LEN = 128

GRID_W = 64
H_HGRN = 4
DK_HGRN = 64
DV_HGRN = 64
HGRN_CHUNK = 32
H_MLA = 8
Q_RANK = 384
KV_RANK = 256
D_NOPE = 64
D_ROPE = 32
D_V = 64
D_QK = D_NOPE + D_ROPE
ROPE_THETA = 10000.0
Q_BLOCK = 128
G_FNET = 4
C_FNET = 64
W_HGRN = H_HGRN * DV_HGRN
W_MLA = H_MLA * D_V
W_FNET = G_FNET * C_FNET
MIX_WIDTH = W_HGRN + W_MLA + W_FNET
IN_SIZES = (H_HGRN * DK_HGRN, H_HGRN * DK_HGRN, H_HGRN * DK_HGRN, W_HGRN, W_HGRN, Q_RANK, KV_RANK, D_ROPE, W_FNET)
IN_WIDTH = sum(IN_SIZES)
D_FF = 2816
N_MOD = 9
EPS = 1e-6

kernel_name = 'hybrid_hgrn2_mla_fnet_diffusion_step'

def rmsnorm(x, g):
    xf = x.astype(jnp.float32)
    y = xf * lax.rsqrt(jnp.mean(xf * xf, axis=-1, keepdims=True) + EPS)
    return (y * g.astype(jnp.float32)).astype(x.dtype)

def swiglu(h, w_gu, w_down):
    gate, up = jnp.split(h @ w_gu, 2, axis=-1)
    return (jax.nn.silu(gate) * up) @ w_down

def axial_rope_tables(L):
    rows = L // GRID_W
    row = jnp.repeat(jnp.arange(rows, dtype=jnp.float32), GRID_W)
    col = jnp.tile(jnp.arange(GRID_W, dtype=jnp.float32), rows)
    pos = jnp.stack([row, col], axis=-1)
    n_freq = D_ROPE // 4
    freq = ROPE_THETA ** (-jnp.arange(n_freq, dtype=jnp.float32) / n_freq)
    ang = pos[:, :, None] * freq
    return jnp.cos(ang), jnp.sin(ang)

def apply_axial_rope(x, cos, sin):
    shp = x.shape
    xr = x.astype(jnp.float32).reshape(shp[:-1] + (2, 2, D_ROPE // 4))
    x1, x2 = xr[..., 0, :], xr[..., 1, :]
    out = jnp.stack([x1 * cos - x2 * sin, x2 * cos + x1 * sin], axis=-2)
    return out.reshape(shp).astype(x.dtype)

def block_attention(q, k, v):
    B, Lq, H, E = q.shape
    nb = Lq // Q_BLOCK
    scale = E ** -0.5
    qb = q.reshape(B, nb, Q_BLOCK, H, E).transpose(1, 0, 2, 3, 4)

    def attend(qi):
        s = jnp.einsum('bqhe,bkhe->bhqk', qi, k).astype(jnp.float32) * scale
        pr = jax.nn.softmax(s, axis=-1).astype(v.dtype)
        return jnp.einsum('bhqk,bkhd->bqhd', pr, v)

    o = lax.map(attend, qb)
    return o.transpose(1, 0, 2, 3, 4).reshape(B, Lq, H, v.shape[-1])

def hgrn_gates(f_raw, lb):
    x = f_raw.astype(jnp.float32)
    lbf = lb.astype(jnp.float32)
    g = jnp.logaddexp(jnp.log(lbf), jnp.log1p(-lbf) + jax.nn.log_sigmoid(x))
    return g, -jnp.expm1(g)

def hgrn_scan(q, k, v, g, s0):
    B, L, H, DK = q.shape
    DV = v.shape[-1]
    n = L // HGRN_CHUNK

    def chunks(a):
        return a.astype(jnp.float32).reshape(B, n, HGRN_CHUNK, H, a.shape[-1]).transpose(1, 0, 3, 2, 4)

    mask = jnp.tril(jnp.ones((HGRN_CHUNK, HGRN_CHUNK), dtype=bool))[:, :, None]

    def step(S, inp):
        qc, kc, vc, gc = inp
        b = jnp.cumsum(gc, axis=2)
        o_inter = jnp.einsum('bhtk,bhkv->bhtv', qc * jnp.exp(b), S)
        diff = b[:, :, :, None, :] - b[:, :, None, :, :]
        decay = jnp.exp(jnp.where(mask, diff, -jnp.inf))
        scores = jnp.einsum('bhtsk,bhsk->bhts', decay * qc[:, :, :, None, :], kc)
        o_intra = jnp.einsum('bhts,bhsv->bhtv', scores, vc)
        b_last = b[:, :, -1:, :]
        S_new = jnp.exp(b_last[:, :, 0, :])[..., None] * S + jnp.einsum('bhsk,bhsv->bhkv', kc * jnp.exp(b_last - b), vc)
        return S_new, o_inter + o_intra

    S_fin, o = lax.scan(step, s0.astype(jnp.float32), (chunks(q), chunks(k), chunks(v), chunks(g)))
    return o.transpose(1, 0, 3, 2, 4).reshape(B, L, H, DV), S_fin

def mla_query(c_q, l, p, rope):
    B, L, _ = c_q.shape
    q = (rmsnorm(c_q, p['mla_q_norm_g'][l]) @ p['mla_w_q_up'][l]).reshape(B, L, H_MLA, D_QK)
    q = rmsnorm(q, p['mla_qk_norm_g'][l, 0])
    if rope is not None:
        cos, sin = rope
        q = jnp.concatenate([q[..., :D_NOPE], apply_axial_rope(q[..., D_NOPE:], cos[:, None], sin[:, None])], axis=-1)
    return q

def mla_keys(ckv_n, k_r, l, p, rope):
    B, L, _ = ckv_n.shape
    kv = (ckv_n @ p['mla_w_kv_up'][l]).reshape(B, L, H_MLA, D_NOPE + D_V)
    k_nope, v = kv[..., :D_NOPE], kv[..., D_NOPE:]
    k = jnp.concatenate([k_nope, jnp.broadcast_to(k_r[:, :, None, :], (B, L, H_MLA, D_ROPE)).astype(k_nope.dtype)], axis=-1)
    k = rmsnorm(k, p['mla_qk_norm_g'][l, 1])
    if rope is not None:
        cos, sin = rope
        k = jnp.concatenate([k[..., :D_NOPE], apply_axial_rope(k[..., D_NOPE:], cos[:, None], sin[:, None])], axis=-1)
    return k, v

def mixer(h, l, p, lb, cache, rope):
    B, L, _ = h.shape
    u = h @ p['w_in'][l]
    offsets = [int(o) for o in np.cumsum(IN_SIZES)[:-1]]
    q_h, f_fw, f_bw, v_h, gate_h, c_q, c_kv, k_r, u_f = jnp.split(u, offsets, axis=-1)

    def heads(a):
        return a.reshape(B, L, H_HGRN, -1)
    qh = jax.nn.silu(heads(q_h))
    vh = heads(v_h)
    g_f, k_f = hgrn_gates(heads(f_fw), lb[0].reshape(H_HGRN, DK_HGRN))
    g_b, k_b = hgrn_gates(heads(f_bw), lb[1].reshape(H_HGRN, DK_HGRN))
    if cache is None:
        s_f0 = jnp.zeros((B, H_HGRN, DK_HGRN, DV_HGRN), jnp.float32)
        s_b0 = s_f0
    else:
        s_f0, s_b0 = cache[2], cache[3]
    o_f, s_f = hgrn_scan(qh, k_f, vh, g_f, s_f0)
    o_b, s_b = hgrn_scan(jnp.flip(qh, 1), jnp.flip(k_b, 1), jnp.flip(vh, 1), jnp.flip(g_b, 1), s_b0)
    o_h = (o_f + jnp.flip(o_b, 1)).astype(h.dtype)
    o_hgrn = (rmsnorm(o_h, p['hgrn_norm_g'][l]) * jax.nn.silu(heads(gate_h))).reshape(B, L, W_HGRN)

    ckv_n = rmsnorm(c_kv, p['mla_kv_norm_g'][l])
    q = mla_query(c_q, l, p, rope)
    k, v = mla_keys(ckv_n, k_r, l, p, rope)
    if cache is not None:
        k_c, v_c = mla_keys(cache[0], cache[1], l, p, None)
        k = jnp.concatenate([k_c.astype(k.dtype), k], axis=1)
        v = jnp.concatenate([v_c.astype(v.dtype), v], axis=1)
    o_mla = rmsnorm(block_attention(q, k, v).reshape(B, L, W_MLA), p['mla_out_norm_g'][l])

    uf = u_f.astype(jnp.float32).reshape(B, L, G_FNET, C_FNET)
    spec = jnp.fft.fft2(uf, axes=(1, 3), norm='ortho').real.astype(h.dtype)
    o_fn = jnp.einsum('blgc,gcd->blgd', spec, p['fnet_w'][l]).reshape(B, L, W_FNET)
    o_fnet = rmsnorm(o_fn, p['fnet_norm_g'][l])

    out = jnp.concatenate([o_hgrn, o_mla, o_fnet], axis=-1) @ p['w_out'][l]
    return out, (ckv_n, k_r, s_f, s_b)

def layer_block(x, mod, l, p, lb, cache, rope):
    m = jnp.split(mod, N_MOD, axis=-1)
    h = rmsnorm(x, p['norm_g'][l, 0]) * (1 + m[1]) + m[0]
    x = x + 0.5 * m[2] * swiglu(h, p['ffn_w_gu'][l, 0], p['ffn_w_down'][l, 0])
    h = rmsnorm(x, p['norm_g'][l, 1]) * (1 + m[4]) + m[3]
    o, ctx = mixer(h, l, p, lb, cache, rope)
    x = x + m[5] * o
    h = rmsnorm(x, p['norm_g'][l, 2]) * (1 + m[7]) + m[6]
    x = x + 0.5 * m[8] * swiglu(h, p['ffn_w_gu'][l, 1], p['ffn_w_down'][l, 1])
    return x, ctx

def setup_inputs(seed: int = 0) -> dict:
    key = jax.random.key(seed)
    ks = jax.random.split(key, 24)
    f32 = jnp.float32

    def nrm(k, shape, scale):
        return jax.random.normal(k, shape, f32) * scale

    def gain(k, shape):
        return 1.0 + 0.05 * jax.random.normal(k, shape, f32)

    return {
        'x_prompt': nrm(ks[0], (BATCH, SEQ, D_MODEL), 1.0),
        'x_sample': nrm(ks[1], (DEC_BATCH, DEC_SEQ, D_MODEL), 1.0),
        'cache_ckv': nrm(ks[2], (DEC_BATCH, DEPTH, PAST_LEN, KV_RANK), 1.0),
        'cache_krope': nrm(ks[3], (DEC_BATCH, DEPTH, PAST_LEN, D_ROPE), 1.0),
        'state_hgrn': nrm(ks[4], (DEC_BATCH, DEPTH, 2, H_HGRN, DK_HGRN, DV_HGRN), 0.5),
        'c': nrm(ks[5], (DEC_BATCH, D_MODEL), 1.0),
        'c_ctx': nrm(ks[6], (D_MODEL,), 1.0),
        'ada_w': nrm(ks[7], (DEPTH, D_MODEL, N_MOD * D_MODEL), 0.5 * D_MODEL ** -0.5),
        'ada_b': nrm(ks[8], (DEPTH, N_MOD * D_MODEL), 0.01),
        'norm_g': gain(ks[9], (DEPTH, 3, D_MODEL)),
        'ffn_w_gu': nrm(ks[10], (DEPTH, 2, D_MODEL, 2 * D_FF), D_MODEL ** -0.5),
        'ffn_w_down': nrm(ks[11], (DEPTH, 2, D_FF, D_MODEL), D_FF ** -0.5),
        'w_in': nrm(ks[12], (DEPTH, D_MODEL, IN_WIDTH), D_MODEL ** -0.5),
        'hgrn_lb': nrm(ks[13], (DEPTH, 2, H_HGRN * DK_HGRN), 0.5),
        'hgrn_norm_g': gain(ks[14], (DEPTH, DV_HGRN)),
        'mla_q_norm_g': gain(ks[15], (DEPTH, Q_RANK)),
        'mla_w_q_up': nrm(ks[16], (DEPTH, Q_RANK, H_MLA * D_QK), Q_RANK ** -0.5),
        'mla_kv_norm_g': gain(ks[17], (DEPTH, KV_RANK)),
        'mla_w_kv_up': nrm(ks[18], (DEPTH, KV_RANK, H_MLA * (D_NOPE + D_V)), KV_RANK ** -0.5),
        'mla_qk_norm_g': gain(ks[19], (DEPTH, 2, D_QK)),
        'mla_out_norm_g': gain(ks[20], (DEPTH, W_MLA)),
        'fnet_w': nrm(ks[21], (DEPTH, G_FNET, C_FNET, C_FNET), C_FNET ** -0.5),
        'fnet_norm_g': gain(ks[22], (DEPTH, W_FNET)),
        'w_out': nrm(ks[23], (DEPTH, MIX_WIDTH, D_MODEL), MIX_WIDTH ** -0.5),
    }

def reference(x_prompt, x_sample, cache_ckv, cache_krope, state_hgrn, c, c_ctx, ada_w, ada_b, norm_g,
              ffn_w_gu, ffn_w_down, w_in, hgrn_lb, hgrn_norm_g, mla_q_norm_g, mla_w_q_up, mla_kv_norm_g,
              mla_w_kv_up, mla_qk_norm_g, mla_out_norm_g, fnet_w, fnet_norm_g, w_out):
    p = dict(norm_g=norm_g, ffn_w_gu=ffn_w_gu, ffn_w_down=ffn_w_down, w_in=w_in, hgrn_norm_g=hgrn_norm_g,
             mla_q_norm_g=mla_q_norm_g, mla_w_q_up=mla_w_q_up, mla_kv_norm_g=mla_kv_norm_g,
             mla_w_kv_up=mla_w_kv_up, mla_qk_norm_g=mla_qk_norm_g, mla_out_norm_g=mla_out_norm_g,
             fnet_w=fnet_w, fnet_norm_g=fnet_norm_g, w_out=w_out)
    lbs = jnp.cumsum(jax.nn.softmax(hgrn_lb.astype(jnp.float32), axis=0), axis=0)
    lbs = lbs - lbs[:1]
    rope = axial_rope_tables(x_sample.shape[1])

    x_ctx = x_prompt
    x_lat = x_sample
    ckv_list, kr_list, st_list = [], [], []
    for l in range(DEPTH):
        mod_ctx = (jax.nn.silu(c_ctx) @ ada_w[l] + ada_b[l])[None, None, :]
        x_ctx, (ckv, kr, s_f, s_b) = layer_block(x_ctx, mod_ctx, l, p, lbs[l], None, None)
        ckv_list.append(ckv)
        kr_list.append(kr)
        st_list.append(jnp.stack([s_f, s_b], axis=1))

        mod_lat = (jax.nn.silu(c) @ ada_w[l] + ada_b[l])[:, None, :]
        cache_l = (cache_ckv[:, l], cache_krope[:, l], state_hgrn[:, l, 0], state_hgrn[:, l, 1])
        x_lat, _ = layer_block(x_lat, mod_lat, l, p, lbs[l], cache_l, rope)

    new_cache_ckv = jnp.stack(ckv_list, axis=1)
    new_cache_krope = jnp.stack(kr_list, axis=1)
    new_state_hgrn = jnp.stack(st_list, axis=1)
    return (x_ctx, x_lat, new_cache_ckv, new_cache_krope, new_state_hgrn)


_drawn_inputs = setup_inputs


def setup_inputs(seed=0):
    import zlib

    import numpy as np

    out = dict(_drawn_inputs(seed))
    spreads = {}
    factors = {'cache_krope': 3.025,
     'state_hgrn': 8.0,
     'hgrn_norm_g': 8.0,
     'mla_q_norm_g': 8.0,
     'mla_qk_norm_g': 8.0,
     'mla_out_norm_g': 3.492,
     'fnet_norm_g': 5.395}
    for name, (base, spread) in spreads.items():
        noise = np.random.default_rng([zlib.crc32(name.encode()), seed]).standard_normal(out[name].shape)
        drawn = base * np.exp(spread * noise) if base else spread * noise
        out[name] = __import__('jax').numpy.asarray(drawn.astype(out[name].dtype))
    for name, factor in factors.items():
        out[name] = (out[name] * factor).astype(out[name].dtype)
    return out
```

```python
import numpy as np
import concourse.bass as bass
from concourse import mybir
from contextlib import ExitStack

P = 128
D_MODEL = 1024
KT = D_MODEL // P
LAT, CTX, PAST = 512, 128, 128
T = LAT + CTX
HT = T // 2
KEYS = T + PAST
HK = KEYS // 2
DEPTH = 2
D_FF = 2816
FT = D_FF // P
FF_PARTS = (12, 10)
N_MOD = 9
MT = N_MOD * KT
CHUNK = 2048
N_ADA = MT // 2
N_WIN = 9
N_QUP = 2
N_OUT = 4
H_MLA, D_NOPE, D_ROPE, D_V = 8, 64, 32, 64
D_QK = D_NOPE + D_ROPE
Q_RANK, KV_RANK = 384, 256
QT_, KVT = Q_RANK // P, KV_RANK // P
EPS = 1e-6
C = 64
NC_LAT, NC_CTX = LAT // C, CTX // C
NCH = NC_LAT + NC_CTX
NU = 2 * NCH
LEVELS = (1, 2, 4, 8, 16, 32)
N_FFN = sum(p + KT for p in FF_PARTS)
PER_LAYER = N_ADA + 2 * N_FFN + N_WIN + 1 + N_QUP + N_OUT
AT_FFN = (N_ADA, PER_LAYER - N_FFN)
AT_WIN = N_ADA + N_FFN
AT_OUT = AT_WIN + N_WIN + 1 + N_QUP
U_Q, U_F, U_V, U_GATE, U_CQ, U_CKV, U_KR, U_FN, N_U = 0, 2, 6, 8, 10, 13, 15, 16, 18
PK = {}
_at = 0
for _name, _n in (("ada_b", MT), ("norm_g", 3 * KT), ("hgrn_g", 1), ("q_g", QT_), ("kv_g", KVT), ("qk_g", 2),
                  ("mla_g", 4), ("fnet_g", 2)):
    PK[_name] = (_at, _n)
    _at += _n
N_PK = _at


MIX_AT = {6: 0, 0: 2, 2: 4}


class Signal:

    def __init__(self, sem, per, first=0):
        self.sem, self.per, self.first = sem, per, first

    def at(self, layer, k):
        return layer * self.per + (k + self.first)


def build(nc, xT, condT, ada_p, params, lb, gu_p, down_a, down_b, win_p, kv_p, q_p, out_p, fnet_w, ckvT, kropeT,
          state, dft, consts, rope, yT, ckv_out, kr_out, state_out):
    fp32, fp32r, u32 = mybir.dt.float32, mybir.dt.float32r, mybir.dt.uint32
    ALU, ACT, AX = mybir.AluOpType, mybir.ActivationFunctionType, mybir.AxisListType

    ctx = ExitStack()
    with ctx:
        def sem(name):
            return ctx.enter_context(nc.semaphore(name))

        def signal(name, per, first=0):
            return Signal(sem(name), per, first)

        def sb(name, shape, dt=fp32):
            return ctx.enter_context(nc.sbuf_tensor(name, shape, dt))

        X = sb("X", [P, KT, T])
        H_hi = sb("H_hi", [P, KT, T], fp32r)
        H_lo = sb("H_lo", [P, KT, T], fp32r)
        raw = [sb(f"raw{i}", [P, CHUNK]) for i in range(2)]
        W_hi = [sb(f"W_hi{i}", [P, CHUNK], fp32r) for i in range(2)]
        W_lo = [sb(f"W_lo{i}", [P, CHUNK], fp32r) for i in range(2)]
        konst = sb("konst", [P, 3 * P + 7 * C + 2 * P + 2])
        ones, pair_ones, ident = (konst[:, i * P:(i + 1) * P] for i in range(3))
        masks = konst[:, 3 * P:3 * P + 7 * C].rearrange("p (m t) -> p m t", m=7)
        chan = konst[:, 3 * P + 7 * C:5 * P + 7 * C]
        add_parts = konst[0:4, 5 * P + 7 * C:5 * P + 7 * C + 2]
        rope_t = sb("rope_t", [P, 2 * LAT + P])
        cos, sin = rope_t[64:96, 0:LAT], rope_t[64:96, LAT:2 * LAT]
        turn = rope_t[0:D_QK, 2 * LAT:2 * LAT + P]
        par = sb("par", [P, N_PK])
        mod = sb("mod", [P, MT, 2])
        up_by = sb("up_by", [P, 3, KT, 2])
        gates = sb("gates", [P, 3, KT, 2])
        cond = sb("cond", [P, KT, 2])
        cond_f = sb("cond_f", [P, KT, 2])
        lbt = sb("lbt", [P, 2, 4])
        lbs = sb("lbs", [P, 2, 4])
        rest = sb("rest", [P, 2, 4])
        lb_l = sb("lb_l", [P, 2, 4])
        eps = sb("eps", [P, 1])
        qk_g = sb("qk_g", [P, 2])
        fw_t = sb("fw_t", [P, 2, P])
        D64 = sb("D64", [P, 2, 2, NCH])
        ckvc = sb("ckvc", [P, KVT, PAST])
        krc = sb("krc", [P, PAST])
        fin_s = sb("fin_s", [P, 2, 2, C])
        nmax = sb("nmax", [P, 8])
        rsum = sb("rsum", [P, 8])
        rinv = sb("rinv", [P, 8])

        R0 = (nc.sbuf_base + 31) // 32 * 32
        ROOM = nc.sbuf_usable_end - R0
        TB, KB = 4 * T, 4 * KEYS

        def at(name, offset, shape, dt=fp32):
            size = 4
            for n in shape[1:]:
                size *= n
            assert offset + size <= ROOM, (name, offset + size, ROOM)
            return nc.alloc_sbuf_tensor_at(name, shape, dt, offset=R0 + offset)

        mod4 = at("mod4", 0, [4, MT * P])
        cond_w = at("cond_w", 4 * MT * P, [P, KT, P], fp32r)
        sq8 = at("sq8", 0, [P, KT, T])
        rsq = at("rsq", 8 * TB, [P, T])
        norm_t = at("norm_t", 9 * TB, [P, KT, T])
        F_hi = at("F_hi", 0, [P, FF_PARTS[0], T], fp32r)
        F_lo = at("F_lo", 12 * TB, [P, FF_PARTS[0], T], fp32r)
        silu_t = at("silu_t", 24 * TB, [P, 2, T])
        ffn_t = at("ffn_t", 26 * TB, [P, 2, T])
        U = at("U", 0, [P, N_U, T])
        E0 = N_U * TB
        dft_t = at("dft_t", E0, [P, 8 * LAT + 2 * P])
        Y = at("Y", E0 + 17408, [P, 5, 4 * P])
        spec = at("spec", E0 + 17408 + 4 * TB, [P, 2, T])
        fsq = at("fsq", E0, [P, 2, T])
        frs = at("frs", E0 + 2 * TB, [P, T])
        fmix = at("fmix", E0 + 3 * TB, [P, 2, T])
        KP = at("KP", E0, [P, 2, 2, T])
        QP = at("QP", E0 + 4 * TB, [P, 2, 2, T])
        A = at("A", E0 + 8 * TB, [P, NU, C])
        Vtok = at("Vtok", E0 + 10 * TB, [P, NU, C])
        D_a = U[:, U_F:U_F + 4, :].rearrange("p (d a) t -> p d (a t)", d=2)
        D_b = at("D_b", E0 + 12 * TB, [P, 2, T])
        S = at("S", E0 + 12 * TB, [P, 2, 2, NCH, C])
        Ktok = at("Ktok", U_F * TB, [P, 2 * NU, C])
        Kc = [at(f"Kc{i}", t * TB, [P, 2 * T]) for i, t in enumerate((U_V, U_FN))]
        hsq = at("hsq", E0, [P, 2 * T])
        hrs = at("hrs", E0 + 2 * TB, [P, 2 * T])
        hmix = at("hmix", E0 + 8 * TB, [P, 2, T])
        csq = at("csq", 0, [P, 5, T])
        crs = at("crs", 5 * TB, [P, 2, T])
        ck_hi = at("ck_hi", E0, [P, KVT, KEYS], fp32r)
        ck_lo = at("ck_lo", E0 + 2 * KB, [P, KVT, KEYS], fp32r)
        cq_hi = at("cq_hi", E0 + 4 * KB, [P, QT_, T], fp32r)
        cq_lo = at("cq_lo", E0 + 4 * KB + 3 * TB, [P, QT_, T], fp32r)
        K_t = at("K_t", 0, [D_QK, H_MLA, KEYS])
        V = at("V", 8 * KB, [P, 6, H_MLA * D_V])
        ksq = at("ksq", 12 * KB, [D_QK, 2, KEYS])
        E1 = E0 + 4 * KB + 6 * TB
        kraw = at("kraw", E1, [D_QK, 2, KEYS])
        krs = at("krs", E1 + 2 * KB, [D_QK, 2, KEYS])
        Q_t = at("Q_t", 12 * KB, [D_QK, H_MLA, T])
        qsq = at("qsq", E1, [D_QK, 2, T])
        qraw = at("qraw", E1 + 2 * TB, [D_QK, 2, T])
        qrs = at("qrs", E1 + 4 * TB, [D_QK, 1, T])
        E2 = 12 * KB + 8 * TB
        probs = at("probs", E2, [P, 2, T])
        probs_t = at("probs_t", E2 + 2 * TB, [P, 2, T])
        O_m = at("O_m", E2 + 4 * TB, [P, 4, T])
        osq = at("osq", 0, [P, 4, T])
        ors = at("ors", 4 * TB, [P, T])

        PS = ctx.enter_context(nc.psum_tensor("PS", [P, 8, 512], fp32))
        flat = PS[:, :, :].rearrange("p b n -> p (b n)")
        in_tiles = flat.rearrange("p (u c) -> p u c", c=P)

        landed = [signal(f"weights_landed{i}", 8 * PER_LAYER) for i in range(2)]
        hi_ready = signal("weights_hi_ready", PER_LAYER)
        split_ready = signal("weights_split", PER_LAYER)
        chunk_done = signal("chunk_multiplied", PER_LAYER, 2)
        emptied = signal("chunk_emptied", PER_LAYER, 2)
        const_landed = sem("const_landed")
        setup = signal("setup_step", 0)
        par_landed = signal("par_landed", 64)
        cond_hi = signal("cond_hi", 1)
        cond_hi_done = signal("cond_hi_done", 1)
        cond_ready = signal("cond_split", 1)
        mod_mm = signal("mod_summed", 1)
        mod_ready = signal("mod_ready", 1)
        sq_ready = signal("norm_squares", 3 * KT)
        stat_mm = signal("norm_sums", 3)
        rs_ready = signal("norm_rsqrt", 3)
        scaled = signal("norm_scaled", 3 * KT)
        h_hi = signal("h_hi_ready", 3 * KT)
        h_lo = signal("h_lo_ready", 3 * KT)
        gate_ready = signal("ffn_silu", 2 * FT)
        f_hi = signal("ffn_hi", 2 * FT)
        f_lo = signal("ffn_lo", 2 * FT, 2)
        dft_landed = signal("dft_landed", 16)
        y_mm = signal("fourier_rows", 5)
        y_ready = signal("fourier_rows_copied", 5)
        spec_mm = signal("fourier_spec", 2)
        spec_ready = signal("fourier_spec_copied", 2)
        fn_mm = signal("fourier_out", 2)
        fsq_ready = signal("fourier_squares", 1)
        fstat_mm = signal("fourier_sums", 1)
        frs_ready = signal("fourier_rsqrt", 1)
        mixed = signal("mix_ready", KT)
        mix_hi = signal("mix_hi_ready", KT)
        mix_lo = signal("mix_lo_ready", KT)
        gates_ready = signal("hgrn_gates", 1)
        vt_mm = signal("hgrn_v_turned", 1)
        v_tok = signal("hgrn_v_ready", 1)
        lev_ready = signal("level_ready", 2 + len(LEVELS))
        lev_mm = signal("level_scores", 1 + len(LEVELS))
        merged = signal("level_merged", 1 + len(LEVELS))
        kt_mm = signal("hgrn_k_turned", 1)
        k_tok = signal("hgrn_k_ready", 1)
        kv_mm = signal("hgrn_kv", 1)
        s0_landed = signal("state_landed", 32)
        s_ready = signal("states_ready", 1)
        o_mm = signal("hgrn_out", 1)
        hsq_ready = signal("hgrn_squares", 1)
        hstat_mm = signal("hgrn_sums", 1)
        hrs_ready = signal("hgrn_rsqrt", 1)
        csq_ready = signal("latent_squares", 1)
        cstat_mm = signal("latent_sums", 1)
        crs_ready = signal("latent_rsqrt", 1)
        c_normed = signal("latent_normed", 1)
        c_hi = signal("latent_hi", 1)
        c_lo = signal("latent_lo", 1)
        stored = signal("cache_stored", 48)
        q_ready = signal("queries_ready", 1)
        heads = {}
        for kind in "kq":
            for what in ("proj", "copied", "squares", "sums", "rsqrt", "normed", "turned_mm", "turned"):
                heads[kind, what] = signal(f"{kind}_{what}", H_MLA)
        v_mm = signal("v_rows", 6)
        v_ready = signal("v_rows_copied", 6)
        UNITS = [(h, t) for h in range(H_MLA) for t in range(5)]
        sc_mm = signal("scores", len(UNITS))
        max_ready = signal("scores_max", len(UNITS))
        exp_ready = signal("probs_exp", len(UNITS))
        p_ready = signal("probs_scaled", len(UNITS))
        pt_mm = signal("probs_turned", len(UNITS))
        pt_ready = signal("probs_t_ready", len(UNITS))
        pv_mm = signal("attn_out", len(UNITS))
        om_ready = signal("attn_out_copied", len(UNITS))
        osq_ready = signal("mla_squares", 1)
        ostat_mm = signal("mla_sums", 1)
        ors_ready = signal("mla_rsqrt", 1)
        y_stored = sem("y_stored")
        wait_passed = sem("wait_passed")

        block = ctx.enter_context(nc.Block())

        def col(name, k=0):
            return par[:, PK[name][0] + k:PK[name][0] + k + 1]

        def halves(bank, n=HT, rows=slice(0, P)):
            return PS[rows, bank:bank + 2, 0:n]

        def two(ap, n=HT):
            return ap.rearrange("p (j n) -> p j n", n=n)

        def flip(t, first, m):
            f = t[:, 0:1, 0:1, first * m:first * m + 1]
            step = 2 * T + (m if first == 0 else -m)
            return bass.AP(f.tensor, f.offset, [list(f.ap[0]), [step, 2], [2 * m, T // m], [1, m]])

        def each(t, first, n, m):
            f = t[:, 0:1, first:first + 1]
            step = t.shape[2] + (1 if first == 0 else -1)
            return bass.AP(f.tensor, f.offset, [list(f.ap[0]), [step, 2], [2, n], [0, m]])

        def pick(t, m, u, rows):
            f = t[rows, 1:2, u // NCH:u // NCH + 1, u % NCH * C:u % NCH * C + 1]
            return bass.AP(f.tensor, f.offset, [list(f.ap[0]), [2 * m, C // (2 * m)], [m - 2 * T, 2], [1, m]])

        def merge(t, m):
            f = t[:, 0:1]
            return bass.AP(f.tensor, f.offset, [list(f.ap[0]), [m, 2], [2 * m, T // m], [1, m]])

        GROUPS = ((0, 0, HT, 0), (1, HT, LAT, 0), (1, LAT, T, 1))

        def alternate(units):
            banks = sorted({u // 8 for u in range(units)})
            order = []
            n = len(banks)
            for i in range(n):
                for r, b in ((0, banks[i]), (1, banks[(i + 1) % n])):
                    order.append((r, [u for u in range(units) if u // 8 == b]))
            return order

        @block.sync
        def _(sp):
            def load(l, c, p, src, size):
                sp.wait_ge(split_ready.sem, split_ready.at(l, c - 1))
                sp.dma_start(raw[p][:, 0:size], src).then_inc(landed[p].sem, 16)

            for p in range(2):
                sp.dma_start(raw[p][:, :], ada_p[p]).then_inc(landed[p].sem, 16)
            with sp.Fori(0, DEPTH) as l:
                with sp.Fori(1, N_ADA // 2) as i:
                    for p in range(2):
                        load(l, 2 * i + p, p, ada_p[l * N_ADA + 2 * i + p], CHUNK)

                def load_ffn(f, c):
                    done = 0
                    for part, down in zip(FF_PARTS, (down_a, down_b)):
                        with sp.Fori(0, part // 2) as i:
                            for p in range(2):
                                load(l, 2 * i + (c + p), p, gu_p[(2 * l + f) * FT + 2 * i + (done + p)], CHUNK)
                        done += part
                        c += part
                        with sp.Fori(0, KT // 2) as i:
                            for p in range(2):
                                load(l, 2 * i + (c + p), p, down[(2 * l + f) * KT + 2 * i + p], part * P)
                        c += KT

                load_ffn(0, AT_FFN[0])
                with sp.Fori(0, 4) as i:
                    for p in range(2):
                        load(l, 2 * i + (AT_WIN + p), p, win_p[l * N_WIN + 2 * i + p], CHUNK)
                load(l, AT_WIN + 8, 0, win_p[l * N_WIN + 8], CHUNK)
                load(l, AT_WIN + 9, 1, kv_p[l], CHUNK)
                for p in range(2):
                    load(l, AT_WIN + 10 + p, p, q_p[2 * l + p], QT_ * 4 * P)
                with sp.Fori(0, N_OUT // 2) as i:
                    for p in range(2):
                        load(l, 2 * i + (AT_OUT + p), p, out_p[l * N_OUT + 2 * i + p], CHUNK)
                load_ffn(1, AT_FFN[1])
                for p in range(2):
                    load(l, PER_LAYER + p, p, ada_p[(l + 1) * N_ADA + p], CHUNK)
            sp.wait_ge(emptied.sem, emptied.at(DEPTH, 0))
            sp.dma_start(yT, X[:, :, :]).then_inc(y_stored, 16)
            sp.wait_ge(y_stored, 16)
            for p in range(2):
                sp.wait_ge(landed[p].sem, 8 * PER_LAYER * DEPTH + 16)

        @block.gpsimd
        def _(pool):
            with pool.Fori(0, DEPTH) as l:
                for f in range(2):
                    done = 0
                    for part in FF_PARTS:
                        with pool.Fori(0, part // 2) as i:
                            for p in range(2):
                                pool.wait_ge(f_hi.sem, f_hi.at(l, 2 * i + (f * FT + done + p + 1)))
                                pool.tensor_tensor(F_lo[:, bass.ds(2 * i + p, 1), :], ffn_t[:, p:p + 1, :],
                                                   F_hi[:, bass.ds(2 * i + p, 1), :].bitcast(fp32),
                                                   ALU.subtract).then_inc(f_lo.sem, 1)
                        done += part
            pool.wait_ge(f_lo.sem, f_lo.at(DEPTH, 0))

        @block.scalar
        def _(act):
            def split_hi(l, c, p):
                act.wait_ge(landed[p].sem, landed[p].at(l, 8 * (c - p) + 16))
                act.wait_ge(chunk_done.sem, chunk_done.at(l, c - 1))
                act.activation(W_hi[p][:, :], raw[p][:, :], ACT.Copy).then_inc(hi_ready.sem, 1)

            def rsqrt(out, src, width):
                act.activation(out, src, ACT.Ln, bias=eps[0:out.shape[0], :], scale=1.0 / width)
                act.drain()
                return act.activation(out, out, ACT.Exp, scale=-0.5)

            def log_exp_tables():
                act.preload_act_table_set("natural_log_exp_and_others")

            act.sem_inc(f_lo.sem, 2)
            for dst, src in ((konst, consts), (rope_t, rope), (cond, condT), (lbt, lb), (X, xT)):
                act.dma_start(dst[tuple(slice(None) for _ in dst.shape)], src).then_inc(const_landed, 16)
            act.wait_ge(const_landed, 80)
            act.activation(cond_f[:, :, :], cond[:, :, :], ACT.Silu)
            act.wait_ge(setup.sem, 1)
            act.activation(lbs[:, :, :], lbt[:, :, :], ACT.Exp).then_inc(setup.sem, 1)
            act.wait_ge(landed[0].sem, 16)
            act.activation(W_hi[0][:, :], raw[0][:, :], ACT.Copy).then_inc(hi_ready.sem, 1)

            def norm(l, j, c):
                act.wait_ge(emptied.sem, emptied.at(l, c))
                for k in range(KT):
                    act.activation(sq8[:, k, :], X[:, k, :], ACT.Square).then_inc(sq_ready.sem, 1)
                log_exp_tables()
                act.wait_ge(stat_mm.sem, stat_mm.at(l, j + 1))
                rsqrt(two(rsq[:, :]), halves(0), D_MODEL).then_inc(rs_ready.sem, 1)
                for k in range(KT):
                    act.wait_ge(scaled.sem, scaled.at(l, j * KT + k + 1))
                    for g, (a, b) in enumerate(((0, LAT), (LAT, T))):
                        done = act.activation(H_hi[:, k, a:b], norm_t[:, k, a:b], ACT.Identity,
                                              bias=mod[:, 3 * j * KT + k, g:g + 1])
                    done.then_inc(h_hi.sem, 1)

            def ffn(l, f, c):
                done = 0
                for part in FF_PARTS:
                    with act.Fori(0, part // 2) as i:
                        for p in range(2):
                            split_hi(l, 2 * i + (c + p + 1), 1 - p)
                            act.wait_ge(chunk_done.sem, chunk_done.at(l, 2 * i + (c + p + 1)))
                            act.activation(two(silu_t[:, p, :]), halves(4 * p), ACT.Silu).then_inc(gate_ready.sem, 1)
                            act.wait_ge(emptied.sem, emptied.at(l, 2 * i + (c + p + 1)))
                            act.activation(F_hi[:, bass.ds(2 * i + p, 1), :], ffn_t[:, p:p + 1, :],
                                           ACT.Copy).then_inc(f_hi.sem, 1)
                    done += part
                    c += part
                    with act.Fori(0, KT // 2) as i:
                        for p in range(2):
                            split_hi(l, 2 * i + (c + p + 1), 1 - p)
                    c += KT

            def to_hi(l, src, t0, n):
                for k in range(n):
                    act.wait_ge(mixed.sem, mixed.at(l, MIX_AT[t0] + k + 1))
                    act.activation(H_hi[:, t0 + k, :], src[:, k, :], ACT.Copy).then_inc(mix_hi.sem, 1)

            with act.Fori(0, DEPTH) as l:
                act.wait_ge(emptied.sem, emptied.at(l, 0))
                act.dma_start(par[:, :], params[l]).then_inc(par_landed.sem, 16)
                act.dma_start(fw_t[:, :, :], fnet_w[l]).then_inc(par_landed.sem, 16)
                act.dma_start(ckvc[:, :, :], ckvT[l]).then_inc(par_landed.sem, 16)
                act.dma_start(krc[64:96, :], kropeT[l]).then_inc(par_landed.sem, 16)

                act.wait_ge(setup.sem, 4)
                act.wait_ge(cond_hi.sem, cond_hi.at(l, 1))
                act.activation(cond_w[:, :, 0:2], cond_f[:, :, :], ACT.Copy).then_inc(cond_hi_done.sem, 1)
                with act.Fori(0, N_ADA // 2) as i:
                    for p in range(2):
                        split_hi(l, 2 * i + (p + 1), 1 - p)
                        act.wait_ge(chunk_done.sem, chunk_done.at(l, 2 * i + (p + 1)))
                        act.activation(mod4[:, bass.ds(512 * i + 256 * p, 256)], PS[0:4, 4 * p, 0:256],
                                       ACT.Copy).then_inc(emptied.sem, 1)
                act.wait_ge(mod_ready.sem, mod_ready.at(l, 1))
                norm(l, 0, AT_FFN[0])
                ffn(l, 0, AT_FFN[0])

                norm(l, 1, AT_WIN)
                act.wait_ge(h_lo.sem, h_lo.at(l, 2 * KT))
                act.dma_start(dft_t[:, :], dft).then_inc(dft_landed.sem, 16)

                def empty_u(l, c, p, t):
                    act.wait_ge(chunk_done.sem, chunk_done.at(l, c + 1))
                    act.activation(U[:, bass.ds(t, 1), :].rearrange("p o (j n) -> p (o j) n", n=HT), halves(4 * p), ACT.Copy)
                    act.activation(U[:, bass.ds(t + 1, 1), :].rearrange("p o (j n) -> p (o j) n", n=HT), halves(4 * p + 2),
                                   ACT.Copy).then_inc(emptied.sem, 1)

                with act.Fori(0, 4) as i:
                    for p in range(2):
                        split_hi(l, 2 * i + (AT_WIN + p + 1), 1 - p)
                        empty_u(l, 2 * i + (AT_WIN + p), p, 4 * i + 2 * p)
                split_hi(l, AT_WIN + 9, 1)
                empty_u(l, AT_WIN + 8, 0, U_FN)
                split_hi(l, AT_WIN + 10, 0)

                for g in range(2):
                    act.wait_ge(spec_mm.sem, spec_mm.at(l, g + 1))
                    act.activation(spec[:, g, 0:LAT], PS[:, 5 + g, :], ACT.Copy)
                    act.activation(spec[:, g, LAT:T], PS[:, 7, g * P:(g + 1) * P], ACT.Copy).then_inc(spec_ready.sem, 1)
                for g in range(2):
                    act.wait_ge(fn_mm.sem, fn_mm.at(l, g + 1))
                    sq = act.activation(two(fsq[:, g, :]), halves(2 * g), ACT.Square)
                sq.then_inc(fsq_ready.sem, 1)
                log_exp_tables()
                act.wait_ge(fstat_mm.sem, fstat_mm.at(l, 1))
                rsqrt(two(frs[:, :]), halves(4), 2 * P).then_inc(frs_ready.sem, 1)
                to_hi(l, fmix, 6, 2)

                act.wait_ge(mix_lo.sem, mix_lo.at(l, 2))
                for t in (U_Q, U_GATE):
                    act.activation(U[:, t:t + 2, :], U[:, t:t + 2, :], ACT.Silu)
                act.activation(KP[:, :, :, :].rearrange("p d a t -> p (d a) t"), U[:, U_F:U_F + 4, :], ACT.Sigmoid, scale=-1.0)
                act.drain()
                act.activation(U[:, U_F:U_F + 4, :], U[:, U_F:U_F + 4, :], ACT.Sigmoid).then_inc(gates_ready.sem, 1)
                act.wait_ge(vt_mm.sem, vt_mm.at(l, 1))
                act.activation(Vtok[:, :, :].rearrange("p u v -> p (u v)"), flat[:, 0:NU * C],
                               ACT.Copy).then_inc(v_tok.sem, 1)
                act.wait_ge(lev_ready.sem, lev_ready.at(l, 2 + len(LEVELS)))
                act.dma_start(S[:, 0, :, 0, :], state[l, :, 0]).then_inc(s0_landed.sem, 16)
                act.dma_start(S[:, 1, :, NC_LAT - 1, :], state[l, :, 1]).then_inc(s0_landed.sem, 16)
                act.wait_ge(kt_mm.sem, kt_mm.at(l, 1))
                act.activation(Ktok[:, :, :].rearrange("p u v -> p (u v)"), flat[:, 0:2 * NU * C],
                               ACT.Copy).then_inc(k_tok.sem, 1)
                act.wait_ge(o_mm.sem, o_mm.at(l, 1))
                act.activation(hsq[:, :], flat[:, 5 * 512:5 * 512 + 2 * T], ACT.Square).then_inc(hsq_ready.sem, 1)
                log_exp_tables()
                act.wait_ge(hstat_mm.sem, hstat_mm.at(l, 1))
                rsqrt(hrs[:, :], flat[:, 0:2 * T], C).then_inc(hrs_ready.sem, 1)
                to_hi(l, hmix, 0, 2)

                act.wait_ge(mix_lo.sem, mix_lo.at(l, 4))
                act.activation(csq[:, :, :], U[:, U_CQ:U_CQ + 5, :], ACT.Square).then_inc(csq_ready.sem, 1)
                act.wait_ge(cstat_mm.sem, cstat_mm.at(l, 1))
                rsqrt(two(crs[:, 0, :]), halves(0), Q_RANK)
                rsqrt(two(crs[:, 1, :]), halves(2), KV_RANK).then_inc(crs_ready.sem, 1)
                act.wait_ge(c_normed.sem, c_normed.at(l, 1))
                act.activation(cq_hi[:, :, :], U[:, U_CQ:U_CQ + QT_, :], ACT.Copy)
                act.activation(ck_hi[:, :, 0:T], U[:, U_CKV:U_CKV + KVT, :], ACT.Copy)
                act.activation(ck_hi[:, :, T:KEYS], ckvc[:, :, :], ACT.Copy).then_inc(c_hi.sem, 1)
                act.dma_start(ckv_out[l], U[:, U_CKV:U_CKV + KVT, LAT:T]).then_inc(stored.sem, 16)
                act.dma_start(kr_out[l], U[64:96, U_KR, LAT:T]).then_inc(stored.sem, 16)
                act.dma_start(state_out[l], fin_s[:, :, :, :]).then_inc(stored.sem, 16)
                act.wait_ge(stored.sem, stored.at(l, 48))

                def squares(l, kind, h):
                    sg = {what: heads[kind, what] for what in ("copied", "squares", "proj")}
                    if kind == "k":
                        act.wait_ge(sg["copied"].sem, sg["copied"].at(l, h + 1))
                        act.activation(ksq[:, h % 2, :], kraw[:, h % 2, :], ACT.Square).then_inc(sg["squares"].sem, 1)
                    else:
                        act.wait_ge(sg["proj"].sem, sg["proj"].at(l, h + 1))
                        src = halves(2 * (h % 2), rows=slice(0, D_QK))
                        if h >= 2:
                            act.wait_ge(heads["q", "normed"].sem, heads["q", "normed"].at(l, h - 1))
                        act.activation(two(qraw[:, h % 2, :]), src, ACT.Copy).then_inc(sg["copied"].sem, 1)
                        act.activation(two(qsq[:, h % 2, :]), src, ACT.Square).then_inc(sg["squares"].sem, 1)

                def head_rsqrt(l, kind, h):
                    n = HK if kind == "k" else HT
                    out = krs[:, h % 2, :] if kind == "k" else qrs[:, 0, :]
                    act.wait_ge(heads[kind, "sums"].sem, heads[kind, "sums"].at(l, h + 1))
                    before = h - 1 if kind == "k" else h
                    if before >= 1:
                        act.wait_ge(heads[kind, "normed"].sem, heads[kind, "normed"].at(l, before))
                    rsqrt(two(out, n), halves(4, n, slice(0, D_QK)), D_QK).then_inc(heads[kind, "rsqrt"].sem, 1)

                for h in range(H_MLA + 1):
                    if h < H_MLA:
                        squares(l, "k", h)
                    if h >= 1:
                        head_rsqrt(l, "k", h - 1)
                split_hi(l, AT_WIN + 11, 1)
                act.wait_ge(emptied.sem, emptied.at(l, AT_WIN + 10))
                for h in range(H_MLA + 1):
                    if h < H_MLA:
                        squares(l, "q", h)
                    if h >= 1:
                        head_rsqrt(l, "q", h - 1)
                    if h == 5:
                        split_hi(l, AT_OUT, 0)

                def exp(l, u):
                    w = T if UNITS[u][1] < 4 else CTX
                    act.wait_ge(max_ready.sem, max_ready.at(l, u + 1))
                    if u >= 2:
                        act.wait_ge(pt_mm.sem, pt_mm.at(l, u - 1))
                    act.activation(probs[:, u % 2, 0:w], flat[:, 1024 * (u % 2):1024 * (u % 2) + w], ACT.Exp,
                                   bias=nmax[:, u % 8:u % 8 + 1],
                                   accum_out=rsum[:, u % 8:u % 8 + 1]).then_inc(exp_ready.sem, 1)

                def copy_pt(l, u):
                    w = T if UNITS[u][1] < 4 else CTX
                    act.wait_ge(pt_mm.sem, pt_mm.at(l, u + 1))
                    if u >= 2:
                        act.wait_ge(pv_mm.sem, pv_mm.at(l, u - 1))
                    act.activation(probs_t[:, u % 2, 0:w], flat[:, 2048:2048 + w], ACT.Copy).then_inc(pt_ready.sem, 1)

                for u in range(len(UNITS) + 1):
                    if u >= 1:
                        copy_pt(l, u - 1)
                    if u < len(UNITS):
                        exp(l, u)
                act.wait_ge(om_ready.sem, om_ready.at(l, len(UNITS)))
                act.activation(osq[:, :, :], O_m[:, :, :], ACT.Square).then_inc(osq_ready.sem, 1)
                act.wait_ge(ostat_mm.sem, ostat_mm.at(l, 1))
                rsqrt(two(ors[:, :]), halves(0), H_MLA * D_V).then_inc(ors_ready.sem, 1)
                to_hi(l, O_m, 2, 4)
                with act.Fori(0, N_OUT // 2) as i:
                    for p in range(2):
                        split_hi(l, 2 * i + (AT_OUT + p + 1), 1 - p)

                norm(l, 2, AT_FFN[1])
                ffn(l, 1, AT_FFN[1])

        @block.vector
        def _(dve):
            def split_lo(l, c, p):
                dve.wait_ge(hi_ready.sem, hi_ready.at(l, c + 1))
                dve.tensor_tensor(W_lo[p][:, :], raw[p][:, :], W_hi[p][:, :].bitcast(fp32),
                                  ALU.subtract).then_inc(split_ready.sem, 1)

            dve.sem_inc(chunk_done.sem, 2)
            dve.sem_inc(emptied.sem, 2)
            dve.memset(eps[:, :], EPS)
            dve.wait_ge(const_landed, 80)
            dve.tensor_tensor(rest[:, 0, :], lbt[:, 0, :], lbt[:, 1, :], ALU.max)
            dve.drain()
            for i in range(2):
                done = dve.tensor_tensor(lbt[:, i, :], lbt[:, i, :], rest[:, 0, :], ALU.subtract)
            done.then_inc(setup.sem, 1)
            dve.wait_ge(setup.sem, 2)
            dve.tensor_tensor(lbt[:, 0, :], lbs[:, 0, :], lbs[:, 1, :], ALU.add)
            dve.drain()
            dve.reciprocal(lbt[:, 0, :], lbt[:, 0, :])
            dve.drain()
            dve.tensor_tensor(rest[:, 1, :], lbs[:, 0, :], lbt[:, 0, :], ALU.mult)
            dve.tensor_tensor(lbt[:, 1, :], lbs[:, 1, :], lbt[:, 0, :], ALU.mult)
            dve.memset(rest[:, 0, :], 1.0)
            dve.drain()
            dve.tensor_copy(lbs[:, 1, :], lbt[:, 1, :])
            dve.memset(lbs[:, 0, :], 0.0)
            dve.drain().then_inc(setup.sem, 2)
            dve.wait_ge(hi_ready.sem, 1)
            dve.tensor_tensor(W_lo[0][:, :], raw[0][:, :], W_hi[0][:, :].bitcast(fp32),
                              ALU.subtract).then_inc(split_ready.sem, 1)

            def norm(l, j):
                dve.wait_ge(rs_ready.sem, rs_ready.at(l, j + 1))
                for k in range(KT + 1):
                    if k < KT:
                        for g, (a, b) in enumerate(((0, LAT), (LAT, T))):
                            done = dve.scalar_tensor_tensor(norm_t[:, k, a:b], X[:, k, a:b], up_by[:, j, k, g:g + 1],
                                                            rsq[:, a:b], ALU.mult, ALU.mult)
                        done.then_inc(scaled.sem, 1)
                    if k >= 1:
                        q = k - 1
                        dve.wait_ge(h_hi.sem, h_hi.at(l, j * KT + q + 1))
                        for g, (a, b) in enumerate(((0, LAT), (LAT, T))):
                            done = dve.scalar_tensor_tensor(H_lo[:, q, a:b], norm_t[:, q, a:b],
                                                            mod[:, 3 * j * KT + q, g:g + 1],
                                                            H_hi[:, q, a:b].bitcast(fp32), ALU.add, ALU.subtract)
                        done.then_inc(h_lo.sem, 1)

            def add_to_x(r, k, bank):
                for j, a, b, g in GROUPS:
                    xs = X[:, bass.ds(k, 1), a:b].rearrange("p o n -> p (o n)")
                    done = dve.scalar_tensor_tensor(xs, PS[:, bank + j, a - HT * j:b - HT * j],
                                                    gates[:, r, bass.ds(k, 1), g:g + 1].rearrange("p o g -> p (o g)"),
                                                    xs, ALU.mult, ALU.add)
                return done

            def ffn(l, f, c):
                done = 0
                for part in FF_PARTS:
                    with dve.Fori(0, part // 2) as i:
                        for p in range(2):
                            split_lo(l, 2 * i + (c + p + 1), 1 - p)
                            dve.wait_ge(gate_ready.sem, gate_ready.at(l, 2 * i + (f * FT + done + p + 1)))
                            dve.wait_ge(f_lo.sem, f_lo.at(l, 2 * i + (f * FT + done + p - 1)))
                            dve.tensor_tensor(two(ffn_t[:, p, :]), two(silu_t[:, p, :]), halves(4 * p + 2),
                                              ALU.mult).then_inc(emptied.sem, 1)
                    done += part
                    c += part
                    with dve.Fori(0, KT // 2) as i:
                        for p in range(2):
                            split_lo(l, 2 * i + (c + p + 1), 1 - p)
                            dve.wait_ge(chunk_done.sem, chunk_done.at(l, 2 * i + (c + p + 1)))
                            add_to_x(2 * f, 2 * i + p, 4 * p).then_inc(emptied.sem, 1)
                            dve.drain()
                    c += KT

            def to_lo(l, src, t0, n):
                for k in range(n):
                    dve.wait_ge(mix_hi.sem, mix_hi.at(l, MIX_AT[t0] + k + 1))
                    dve.tensor_tensor(H_lo[:, t0 + k, :], src[:, k, :], H_hi[:, t0 + k, :].bitcast(fp32),
                                      ALU.subtract).then_inc(mix_lo.sem, 1)

            with dve.Fori(0, DEPTH) as l:
                dve.wait_ge(emptied.sem, emptied.at(l, 0))
                dve.memset(cond_w[:, :, :].bitcast(fp32), 0.0)
                dve.tensor_copy(lb_l[:, 0:1, :], lbs[:, bass.ds(l, 1), :])
                dve.tensor_copy(lb_l[:, 1:2, :], rest[:, bass.ds(l, 1), :])
                dve.drain().then_inc(cond_hi.sem, 1)
                dve.wait_ge(cond_hi_done.sem, cond_hi_done.at(l, 1))
                dve.tensor_tensor(cond_w[:, :, 2:4], cond_f[:, :, :], cond_w[:, :, 0:2].bitcast(fp32),
                                  ALU.subtract).then_inc(cond_ready.sem, 1)
                with dve.Fori(0, N_ADA // 2) as i:
                    for p in range(2):
                        split_lo(l, 2 * i + (p + 1), 1 - p)
                dve.wait_ge(par_landed.sem, par_landed.at(l, 64))
                dve.wait_ge(mod_mm.sem, mod_mm.at(l, 1))
                b0 = PK["ada_b"][0]
                for g in range(2):
                    dve.tensor_tensor(mod[:, :, g], PS[:, 7, g:2 * MT:2], par[:, b0:b0 + MT], ALU.add)
                dve.drain()
                g0 = PK["norm_g"][0]
                for j in range(3):
                    for g in range(2):
                        dve.scalar_tensor_tensor(up_by[:, j, :, g], mod[:, (3 * j + 1) * KT:(3 * j + 2) * KT, g], 1.0,
                                                 par[:, g0 + j * KT:g0 + (j + 1) * KT], ALU.add, ALU.mult)
                    dve.tensor_scalar(gates[:, j, :, :], mod[:, (3 * j + 2) * KT:(3 * j + 3) * KT, :],
                                      1.0 if j == 1 else 0.5, None, ALU.mult)
                qk = PK["qk_g"][0]
                dve.tensor_scalar(qk_g[0:D_QK, 0:1], par[0:D_QK, qk:qk + 1], float(D_QK) ** -0.5, None, ALU.mult)
                dve.tensor_copy(qk_g[0:D_QK, 1:2], par[0:D_QK, qk + 1:qk + 2])
                dve.drain().then_inc(mod_ready.sem, 1)
                norm(l, 0)
                ffn(l, 0, AT_FFN[0])

                norm(l, 1)
                with dve.Fori(0, 4) as i:
                    for p in range(2):
                        split_lo(l, 2 * i + (AT_WIN + p + 1), 1 - p)
                split_lo(l, AT_WIN + 9, 1)
                split_lo(l, AT_WIN + 10, 0)

                for t in range(5):
                    dve.wait_ge(y_mm.sem, y_mm.at(l, t + 1))
                    dve.tensor_copy(Y[:, t, :], PS[:, t, :]).then_inc(y_ready.sem, 1)
                dve.wait_ge(frs_ready.sem, frs_ready.at(l, 1))
                for g in range(2):
                    dve.scalar_tensor_tensor(two(fmix[:, g, :]), halves(2 * g), col("fnet_g", g), two(frs[:, :]),
                                             ALU.mult, ALU.mult).then_inc(mixed.sem, 1)
                to_lo(l, fmix, 6, 2)

                dve.wait_ge(gates_ready.sem, gates_ready.at(l, 1))
                for d in range(2):
                    for a in range(2):
                        n = 2 * d + a
                        dve.tensor_scalar(KP[:, d, a, :], KP[:, d, a, :], lb_l[:, 1, n:n + 1], None, ALU.mult)
                        dve.tensor_scalar(U[:, U_F + n, :], U[:, U_F + n, :], lb_l[:, 1, n:n + 1], lb_l[:, 0, n:n + 1],
                                          ALU.mult, ALU.add)
                dve.drain()
                for d in range(2):
                    dve.tensor_tensor(QP[:, d, :, :], U[:, U_Q:U_Q + 2, :], U[:, U_F + 2 * d:U_F + 2 * d + 2, :], ALU.mult)
                dve.wait_ge(vt_mm.sem, vt_mm.at(l, 1))
                dve.tensor_tensor(Kc[0][:, :], KP[:, 0, :, :].rearrange("p a t -> p (a t)"),
                                  KP[:, 1, :, :].rearrange("p a t -> p (a t)"), ALU.add)
                dve.tensor_copy(merge(Kc[1], 1), flip(KP, 0, 1))
                dve.drain().then_inc(lev_ready.sem, 2)

                decay = D_a
                for li in range(1 + len(LEVELS)):
                    if li >= 1:
                        m = LEVELS[li - 1]
                        nb = 2 * T // m
                        dve.tensor_tensor(flip(KP, 0, m), flip(KP, 0, m), each(decay, 1, nb // 2, m), ALU.mult)
                        if li < len(LEVELS):
                            dve.drain()
                            dve.tensor_copy(merge(Kc[(li + 1) % 2], 2 * m), flip(KP, 0, 2 * m))
                    dve.wait_ge(lev_mm.sem, lev_mm.at(l, li + 1))
                    if li >= 1:
                        dve.tensor_tensor(flip(QP, 1, m), flip(QP, 1, m), each(decay, 0, nb // 2, m), ALU.mult)
                        if m == LEVELS[-1]:
                            nxt = D64[:, :, :, :].rearrange("p d a c -> p d (a c)")
                        else:
                            nxt = (D_b if decay is D_a else D_a)[:, :, 0:nb // 2]
                        pairs = decay[:, :, 0:nb].rearrange("p d (n two) -> p d n two", two=2)
                        dve.tensor_tensor(nxt, pairs[:, :, :, 0], pairs[:, :, :, 1], ALU.mult)
                        dve.drain().then_inc(lev_ready.sem, 1)
                        decay = D_b if decay is D_a else D_a
                    scores = flat[:, 1536 * (li % 2):1536 * (li % 2) + 2 * T].rearrange("p (u t) -> p u t", t=C)
                    mask = masks[:, li:li + 1, :].to_broadcast([P, NU, C])
                    if li == 0:
                        dve.tensor_tensor(A[:, :, :], scores, mask, ALU.mult).then_inc(merged.sem, 1)
                    else:
                        dve.copy_predicated(A[:, :, :], mask.bitcast(u32), scores).then_inc(merged.sem, 1)
                    dve.drain()

                kv = flat[:, 0:2 * NU * C].rearrange("p (d a c v) -> p d a c v", d=2, a=2, c=NCH)
                dve.wait_ge(kv_mm.sem, kv_mm.at(l, 1))
                dve.wait_ge(s0_landed.sem, s0_landed.at(l, 32))

                def carry(d, a, frm, dst):
                    src = S[:, d, a, frm, :]
                    dve.scalar_tensor_tensor(dst, src, D64[:, d, a, frm:frm + 1], kv[:, d, a, frm, :], ALU.mult, ALU.add)

                last_c = NCH - 1
                for r in range(NC_LAT - 1):
                    for a in range(2):
                        carry(0, a, r, S[:, 0, a, r + 1, :])
                        carry(1, a, NC_LAT - 1 - r, S[:, 1, a, NC_LAT - 2 - r, :])
                        if r == 0:
                            dve.tensor_copy(S[:, 0, a, last_c, :], kv[:, 0, a, NC_LAT, :])
                            dve.tensor_copy(S[:, 1, a, NC_LAT, :], kv[:, 1, a, last_c, :])
                        if r == 1:
                            carry(0, a, last_c, fin_s[:, 0, a, :])
                            carry(1, a, NC_LAT, fin_s[:, 1, a, :])
                    dve.drain()
                dve.drain().then_inc(s_ready.sem, 1)
                dve.wait_ge(hrs_ready.sem, hrs_ready.at(l, 1))
                dve.scalar_tensor_tensor(hmix[:, :, :].rearrange("p a t -> p (a t)"), flat[:, 5 * 512:5 * 512 + 2 * T],
                                         col("hgrn_g"), hrs[:, :], ALU.mult, ALU.mult)
                dve.drain()
                for a in range(2):
                    dve.tensor_tensor(hmix[:, a, :], hmix[:, a, :], U[:, U_GATE + a, :], ALU.mult).then_inc(mixed.sem, 1)
                to_lo(l, hmix, 0, 2)

                dve.wait_ge(crs_ready.sem, crs_ready.at(l, 1))
                for k in range(QT_):
                    dve.scalar_tensor_tensor(U[:, U_CQ + k, :], U[:, U_CQ + k, :], col("q_g", k), crs[:, 0, :],
                                             ALU.mult, ALU.mult)
                for k in range(KVT):
                    dve.scalar_tensor_tensor(U[:, U_CKV + k, :], U[:, U_CKV + k, :], col("kv_g", k), crs[:, 1, :],
                                             ALU.mult, ALU.mult)
                for b in range(2):
                    dve.tensor_copy(kraw[64:96, b, 0:T], U[64:96, U_KR, :])
                    dve.tensor_copy(kraw[64:96, b, T:KEYS], krc[64:96, :])
                dve.drain().then_inc(c_normed.sem, 1)
                dve.wait_ge(c_hi.sem, c_hi.at(l, 1))
                dve.tensor_tensor(cq_lo[:, :, :], U[:, U_CQ:U_CQ + QT_, :], cq_hi[:, :, :].bitcast(fp32), ALU.subtract)
                dve.tensor_tensor(ck_lo[:, :, 0:T], U[:, U_CKV:U_CKV + KVT, :], ck_hi[:, :, 0:T].bitcast(fp32), ALU.subtract)
                dve.tensor_tensor(ck_lo[:, :, T:KEYS], ckvc[:, :, :], ck_hi[:, :, T:KEYS].bitcast(fp32),
                                  ALU.subtract).then_inc(c_lo.sem, 1)
                dve.wait_ge(stored.sem, stored.at(l, 48))

                def copy_k(l, h):
                    if h:
                        dve.drain()
                    dve.wait_ge(heads["k", "proj"].sem, heads["k", "proj"].at(l, h + 1))
                    dve.tensor_copy(two(kraw[0:D_NOPE, h % 2, :], HK), halves(2 * (h % 2), HK, slice(0, D_NOPE)))\
                       .then_inc(heads["k", "copied"].sem, 1)

                def norm_head(l, kind, h):
                    dve.wait_ge(heads[kind, "rsqrt"].sem, heads[kind, "rsqrt"].at(l, h + 1))
                    if kind == "k":
                        out, src, rs = K_t[:, h, :], kraw[:, h % 2, :], krs[:, h % 2, :]
                    else:
                        out, src, rs = Q_t[:, h, :], qraw[:, h % 2, :], qrs[:, 0, :]
                    g = 1 if kind == "k" else 0
                    dve.scalar_tensor_tensor(out, src, qk_g[0:D_QK, g:g + 1], rs, ALU.mult, ALU.mult)\
                       .then_inc(heads[kind, "normed"].sem, 1)

                def turn_head(l, kind, h):
                    dst = (K_t if kind == "k" else Q_t)[64:96, h, 0:LAT]
                    tmp = PS[64:96, 6, :]
                    dve.wait_ge(heads[kind, "turned_mm"].sem, heads[kind, "turned_mm"].at(l, h + 1))
                    dve.tensor_tensor(tmp, tmp, sin, ALU.mult)
                    dve.tensor_tensor(dst, dst, cos, ALU.mult)
                    dve.drain()
                    dve.tensor_tensor(dst, dst, tmp, ALU.add).then_inc(heads[kind, "turned"].sem, 1)

                for h in range(H_MLA + 3):
                    if 2 <= h < H_MLA + 2:
                        norm_head(l, "k", h - 2)
                    if h < H_MLA:
                        copy_k(l, h)
                    if h >= 3:
                        turn_head(l, "k", h - 3)
                for t in range(6):
                    dve.wait_ge(v_mm.sem, v_mm.at(l, t + 1))
                    dve.tensor_copy(V[:, t, :], PS[:, t % 4, :]).then_inc(v_ready.sem, 1)
                dve.drain().then_inc(emptied.sem, 1)
                split_lo(l, AT_WIN + 11, 1)
                for h in range(H_MLA + 3):
                    if 2 <= h < H_MLA + 2:
                        norm_head(l, "q", h - 2)
                    if h >= 3:
                        turn_head(l, "q", h - 3)
                    if h in (5, 9):
                        dve.drain().then_inc(emptied.sem, 1)
                    if h == 6:
                        split_lo(l, AT_OUT, 0)
                dve.drain().then_inc(q_ready.sem, 1)

                def row_max(l, u):
                    w = T if UNITS[u][1] < 4 else CTX
                    dve.wait_ge(sc_mm.sem, sc_mm.at(l, u + 1))
                    dve.tensor_reduce(nmax[:, u % 8:u % 8 + 1], flat[:, 1024 * (u % 2):1024 * (u % 2) + w], AX.X, ALU.max,
                                      negate=True).then_inc(max_ready.sem, 1)

                def scale_probs(l, u):
                    w = T if UNITS[u][1] < 4 else CTX
                    dve.wait_ge(exp_ready.sem, exp_ready.at(l, u + 1))
                    dve.reciprocal(rinv[:, u % 8:u % 8 + 1], rsum[:, u % 8:u % 8 + 1])
                    dve.drain()
                    dve.tensor_scalar(probs[:, u % 2, 0:w], probs[:, u % 2, 0:w], rinv[:, u % 8:u % 8 + 1], None,
                                      ALU.mult).then_inc(p_ready.sem, 1)

                def copy_om(l, u):
                    h, t = UNITS[u]
                    rows = slice(C * (h % 2), C * (h % 2) + C)
                    dve.wait_ge(pv_mm.sem, pv_mm.at(l, u + 1))
                    dve.tensor_copy(O_m[rows, h // 2, t * P:(t + 1) * P], PS[rows, 6 + u % 2, 0:P]).then_inc(om_ready.sem, 1)

                n = len(UNITS)
                for u in range(n + 2):
                    if 1 <= u <= n:
                        scale_probs(l, u - 1)
                    if u < n:
                        row_max(l, u)
                    if u >= 2:
                        copy_om(l, u - 2)
                dve.wait_ge(ors_ready.sem, ors_ready.at(l, 1))
                for k in range(4):
                    dve.scalar_tensor_tensor(O_m[:, k, :], O_m[:, k, :], col("mla_g", k), ors[:, :], ALU.mult,
                                             ALU.mult).then_inc(mixed.sem, 1)
                to_lo(l, O_m, 2, 4)
                with dve.Fori(0, N_OUT // 2) as i:
                    for p in range(2):
                        split_lo(l, 2 * i + (AT_OUT + p + 1), 1 - p)
                        dve.wait_ge(chunk_done.sem, chunk_done.at(l, 2 * i + (AT_OUT + p + 1)))
                        add_to_x(1, 4 * i + 2 * p, 4 * p)
                        add_to_x(1, 4 * i + (2 * p + 1), 4 * p + 2).then_inc(emptied.sem, 1)
                        dve.drain()

                norm(l, 2)
                ffn(l, 1, AT_FFN[1])

        @block.tensor
        def _(pe):
            def mm(out, lhs, rhs, start, stop):
                return nc.tensor.matmul(out, lhs, rhs, start=start, stop=stop)

            def split_product(outs, lhs, rhs, kts, before=None):
                n = 3 * kts
                for j, out in enumerate(outs):
                    at_ = 0
                    for k in range(kts):
                        if before and j == 0 and k == before[0]:
                            pe.wait_ge(before[1], before[2])
                        (w1, w2), (h1, h2) = lhs(k), rhs(k, j)
                        for w, h in ((w1, h1), (w2, h1), (w1, h2)):
                            last = mm(out, w, h, at_ == 0, at_ == n - 1)
                            at_ += 1
                return last

            def hold():
                pe.sem_inc(wait_passed, 1)

            def begin(l, c):
                pe.wait_ge(split_ready.sem, split_ready.at(l, c + 1))
                pe.wait_ge(emptied.sem, emptied.at(l, c - 1))

            def weights(p, off, step=0):
                return lambda k: (W_hi[p][:, off + k * step:off + k * step + P], W_lo[p][:, off + k * step:off + k * step + P])

            def h_tile(k, j):
                return H_hi[:, k, j * HT:(j + 1) * HT], H_lo[:, k, j * HT:(j + 1) * HT]

            def f_tile(k, j):
                return F_hi[:, k, j * HT:(j + 1) * HT], F_lo[:, k, j * HT:(j + 1) * HT]

            def outs(bank, n=HT, rows=slice(0, P)):
                return [PS[rows, bank + j, 0:n] for j in range(2)]

            def two_tiles(p):
                split_product(outs(4 * p), weights(p, 0, 2 * P), h_tile, KT)
                return split_product(outs(4 * p + 2), weights(p, P, 2 * P), h_tile, KT)

            def sums(bank, stat, src, n=HT):
                for j in range(2):
                    for k, s in enumerate(src):
                        last = mm(PS[0:stat.shape[1], bank + j, 0:n], stat, s[:, j * n:(j + 1) * n], k == 0, k == len(src) - 1)
                return last

            def norm(l, j):
                for k in range(KT):
                    pe.wait_ge(sq_ready.sem, sq_ready.at(l, j * KT + k + 1))
                    for i in range(2):
                        last = mm(PS[:, i, 0:HT], ones, sq8[:, k, i * HT:(i + 1) * HT], k == 0, k == KT - 1)
                last.then_inc(stat_mm.sem, 1)

            def first_chunk(l, j, c):
                begin(l, c)
                for k in range(KT):
                    pe.wait_ge(h_lo.sem, h_lo.at(l, j * KT + k + 1))
                    for n in range(4):
                        off = 2 * P * k + P * (n // 2)
                        w = W_hi[0][:, off:off + P], W_lo[0][:, off:off + P]
                        h = h_tile(k, n % 2)
                        for i, (x, y) in enumerate(((w[0], h[0]), (w[1], h[0]), (w[0], h[1]))):
                            last = mm(PS[:, n, 0:HT], x, y, k == 0 and i == 0, k == KT - 1 and i == 2)
                last.then_inc(chunk_done.sem, 1)
                begin(l, c + 1)
                two_tiles(1).then_inc(chunk_done.sem, 1)

            def ffn(l, f, c):
                done = 0
                first_chunk(l, 2 * f, c)
                for part in FF_PARTS:
                    with pe.Fori(0 if done else 1, part // 2) as i:
                        for p in range(2):
                            begin(l, 2 * i + (c + p))
                            two_tiles(p).then_inc(chunk_done.sem, 1)
                    done += part
                    c += part
                    with pe.Fori(0, KT // 2) as i:
                        for p in range(2):
                            begin(l, 2 * i + (c + p))
                            pe.wait_ge(f_lo.sem, f_lo.at(l, f * FT + done - 2))
                            split_product(outs(4 * p), weights(p, 0, P), f_tile, part,
                                          before=(part - 2, f_lo.sem, f_lo.at(l, f * FT + done)))\
                                .then_inc(chunk_done.sem, 1)
                    c += KT

            pe.wait_ge(const_landed, 80)
            with pe.Fori(0, DEPTH) as l:
                pe.wait_ge(cond_ready.sem, cond_ready.at(l, 1))
                hold()
                with pe.Fori(0, N_ADA // 2) as i:
                    for p in range(2):
                        begin(l, 2 * i + p)
                        for k in range(KT):
                            for w in (W_hi, W_lo):
                                last = mm(PS[:, 4 * p, 0:256], cond_w[:, k, :], w[p][:, 256 * k:256 * (k + 1)],
                                          k == 0 and w is W_hi, k == KT - 1 and w is W_lo)
                        last.then_inc(chunk_done.sem, 1)
                pe.wait_ge(emptied.sem, emptied.at(l, N_ADA))
                for t in range(MT):
                    last = mm(PS[:, 7, 2 * t:2 * t + 2], mod4[0:4, t * P:(t + 1) * P], add_parts, True, True)
                last.then_inc(mod_mm.sem, 1)
                norm(l, 0)
                ffn(l, 0, AT_FFN[0])

                norm(l, 1)
                first_chunk(l, 1, AT_WIN)
                with pe.Fori(1, 4) as i:
                    for p in range(2):
                        begin(l, 2 * i + (AT_WIN + p))
                        two_tiles(p).then_inc(chunk_done.sem, 1)
                begin(l, AT_WIN + 8)
                two_tiles(0).then_inc(chunk_done.sem, 1)

                pe.wait_ge(emptied.sem, emptied.at(l, AT_WIN + 9))
                pe.wait_ge(par_landed.sem, par_landed.at(l, 64))
                for t in range(5):
                    for g in range(2):
                        last = mm(PS[:, t, 2 * P * g:2 * P * (g + 1)], U[:, U_FN + g, t * P:(t + 1) * P], chan, True, True)
                    last.then_inc(y_mm.sem, 1)
                pe.wait_ge(dft_landed.sem, dft_landed.at(l, 16))
                pe.wait_ge(y_ready.sem, y_ready.at(l, 5))
                for g in range(2):
                    for t in range(4):
                        for s in range(2):
                            o = (4 * s + t) * LAT
                            mm(PS[:, 5 + g, :], Y[:, t, 2 * P * g + P * s:2 * P * g + P * (s + 1)], dft_t[:, o:o + LAT],
                               t == 0 and s == 0, t == 3 and s == 1)
                    for s in range(2):
                        o = 8 * LAT + s * P
                        last = mm(PS[:, 7, g * P:(g + 1) * P], Y[:, 4, 2 * P * g + P * s:2 * P * g + P * (s + 1)],
                                  dft_t[:, o:o + P], s == 0, s == 1)
                    last.then_inc(spec_mm.sem, 1)
                    if g == 0:
                        pe.wait_ge(spec_ready.sem, spec_ready.at(l, 1))
                for g in range(2):
                    pe.wait_ge(spec_ready.sem, spec_ready.at(l, g + 1))
                    for j in range(2):
                        last = mm(PS[:, 2 * g + j, 0:HT], fw_t[:, g, :], spec[:, g, j * HT:(j + 1) * HT], True, True)
                    last.then_inc(fn_mm.sem, 1)
                pe.wait_ge(fsq_ready.sem, fsq_ready.at(l, 1))
                sums(4, ones, [fsq[:, g, :] for g in range(2)]).then_inc(fstat_mm.sem, 1)

                def turn_units(src, n):
                    hold()
                    for r, units in alternate(n):
                        rows = slice(C * r, C * r + C)
                        for u in units:
                            last = mm(flat[rows, u * C:(u + 1) * C], src[rows, u * C:(u + 1) * C], ident[rows, rows],
                                      True, True)
                    return last

                pe.wait_ge(mix_lo.sem, mix_lo.at(l, 2))
                turn_units(U[:, U_V:U_V + 2, :].rearrange("p a t -> p (a t)"), NU).then_inc(vt_mm.sem, 1)
                pe.wait_ge(v_tok.sem, v_tok.at(l, 1))
                q_raw = U[:, U_Q:U_Q + 2, :].rearrange("p a t -> p (a t)")
                for li in range(1 + len(LEVELS)):
                    pe.wait_ge(lev_ready.sem, lev_ready.at(l, li + 1 if li else 2))
                    if li >= 2:
                        pe.wait_ge(merged.sem, merged.at(l, li - 1))
                    hold()
                    for r, units in alternate(NU):
                        rows = slice(C * r, C * r + C)
                        for u in units:
                            if li == 0:
                                keys, queries = Kc[0][rows, u * C:(u + 1) * C], q_raw[rows, u * C:(u + 1) * C]
                            else:
                                m = LEVELS[li - 1]
                                keys, queries = Kc[li % 2][rows, u * C:(u + 1) * C], pick(QP, m, u, rows)
                            o = 1536 * (li % 2) + u * C
                            last = mm(flat[rows, o:o + C], keys, queries, True, True)
                    last.then_inc(lev_mm.sem, 1)
                pe.wait_ge(lev_ready.sem, lev_ready.at(l, 2 + len(LEVELS)))
                pe.wait_ge(merged.sem, merged.at(l, 1 + len(LEVELS)))
                turn_units(KP[:, :, :, :].rearrange("p d a t -> p (d a t)"), 2 * NU).then_inc(kt_mm.sem, 1)
                pe.wait_ge(k_tok.sem, k_tok.at(l, 1))
                hold()
                for r, units in alternate(2 * NU):
                    rows = slice(C * r, C * r + C)
                    for u in units:
                        last = mm(flat[rows, u * C:(u + 1) * C], Ktok[rows, u, :], Vtok[rows, u % NU, :], True, True)
                last.then_inc(kv_mm.sem, 1)
                pe.wait_ge(s_ready.sem, s_ready.at(l, 1))
                hold()
                for r, units in alternate(NU):
                    rows = slice(C * r, C * r + C)
                    for u in units:
                        a, c = u // NCH, u % NCH
                        out = flat[rows, 5 * 512 + u * C:5 * 512 + (u + 1) * C]
                        parts = [(Vtok[rows, u, :], A[rows, u, :])]
                        for d in range(2):
                            if c == (NC_LAT, NCH - 1)[d]:
                                continue
                            parts.append((S[rows, d, a, c, :], QP[rows, d, a, c * C:(c + 1) * C]))
                        for n, (w, x) in enumerate(parts):
                            last = mm(out, w, x, n == 0, n == len(parts) - 1)
                last.then_inc(o_mm.sem, 1)
                pe.wait_ge(hsq_ready.sem, hsq_ready.at(l, 1))
                for b in range(0, 2 * T, 512):
                    n = min(512, 2 * T - b)
                    last = mm(flat[:, b:b + n], pair_ones, hsq[:, b:b + n], True, True)
                last.then_inc(hstat_mm.sem, 1)

                pe.wait_ge(csq_ready.sem, csq_ready.at(l, 1))
                sums(0, ones, [csq[:, k, :] for k in range(QT_)])
                sums(2, ones, [csq[:, QT_ + k, :] for k in range(KVT)]).then_inc(cstat_mm.sem, 1)
                pe.wait_ge(c_lo.sem, c_lo.at(l, 1))

                def project(l, kind, h):
                    if h >= 2:
                        what = "copied" if kind == "k" else "squares"
                        pe.wait_ge(heads[kind, what].sem, heads[kind, what].at(l, h - 1))
                    if kind == "k":
                        last = split_product(outs(2 * (h % 2), HK), weights(1, P * h, H_MLA * P),
                                             lambda k, j: (ck_hi[:, k, j * HK:(j + 1) * HK], ck_lo[:, k, j * HK:(j + 1) * HK]),
                                             KVT)
                    else:
                        last = split_product(outs(2 * (h % 2)), weights(h // 4, P * (h % 4), 4 * P),
                                             lambda k, j: (cq_hi[:, k, j * HT:(j + 1) * HT], cq_lo[:, k, j * HT:(j + 1) * HT]),
                                             QT_)
                    last.then_inc(heads[kind, "proj"].sem, 1)

                def head_sums(l, kind, h):
                    pe.wait_ge(heads[kind, "squares"].sem, heads[kind, "squares"].at(l, h + 1))
                    if h >= 1:
                        pe.wait_ge(heads[kind, "rsqrt"].sem, heads[kind, "rsqrt"].at(l, h))
                    src, n = (ksq, HK) if kind == "k" else (qsq, HT)
                    sums(4, ones[0:D_QK, 0:D_QK], [src[:, h % 2, :]], n).then_inc(heads[kind, "sums"].sem, 1)

                def exchange(l, kind, h):
                    pe.wait_ge(heads[kind, "normed"].sem, heads[kind, "normed"].at(l, h + 1))
                    if h >= 1:
                        pe.wait_ge(heads[kind, "turned"].sem, heads[kind, "turned"].at(l, h))
                    src = K_t if kind == "k" else Q_t
                    mm(PS[:, 6, :], turn, src[:, h, 0:LAT], True, True).then_inc(heads[kind, "turned_mm"].sem, 1)

                pe.wait_ge(split_ready.sem, split_ready.at(l, AT_WIN + 10))
                for h in range(H_MLA + 3):
                    if h < H_MLA:
                        project(l, "k", h)
                    if 1 <= h <= H_MLA:
                        head_sums(l, "k", h - 1)
                    if h >= 3:
                        exchange(l, "k", h - 3)
                pe.wait_ge(heads["k", "copied"].sem, heads["k", "copied"].at(l, H_MLA))
                v_w = [w[1][:, :].rearrange("p (k h x) -> p k h x", k=KVT, h=H_MLA)[:, :, :, D_NOPE:] for w in (W_hi, W_lo)]
                for t in range(6):
                    if t >= 4:
                        pe.wait_ge(v_ready.sem, v_ready.at(l, t - 3))
                    split_product([PS[:, t % 4, :]], lambda k: (ck_hi[:, k, t * P:(t + 1) * P], ck_lo[:, k, t * P:(t + 1) * P]),
                                  lambda k, j: (v_w[0][:, k], v_w[1][:, k]), KVT).then_inc(v_mm.sem, 1)
                pe.drain().then_inc(chunk_done.sem, 1)
                pe.wait_ge(emptied.sem, emptied.at(l, AT_WIN + 10))
                pe.wait_ge(split_ready.sem, split_ready.at(l, AT_WIN + 11))
                for h in range(H_MLA + 3):
                    if h == 4:
                        pe.wait_ge(split_ready.sem, split_ready.at(l, AT_WIN + 12))
                    if h < H_MLA:
                        project(l, "q", h)
                    if 1 <= h <= H_MLA:
                        head_sums(l, "q", h - 1)
                    if h >= 3:
                        exchange(l, "q", h - 3)
                    if h in (3, 7):
                        pe.drain().then_inc(chunk_done.sem, 1)
                pe.wait_ge(q_ready.sem, q_ready.at(l, 1))

                def scores(l, u):
                    h, t = UNITS[u]
                    if u >= 2:
                        pe.wait_ge(exp_ready.sem, exp_ready.at(l, u - 1))
                    q, b = Q_t[:, h, t * P:(t + 1) * P], 2 * (u % 2)
                    if t < 4:
                        mm(PS[:, b, :], q, K_t[:, h, 0:LAT], True, True)
                        last = mm(PS[:, b + 1, 0:PAST], q, K_t[:, h, T:KEYS], True, True)
                    else:
                        last = mm(PS[:, b, 0:CTX], q, K_t[:, h, LAT:T], True, True)
                    last.then_inc(sc_mm.sem, 1)

                def turn_probs(l, u):
                    pe.wait_ge(p_ready.sem, p_ready.at(l, u + 1))
                    if u >= 1:
                        pe.wait_ge(pt_ready.sem, pt_ready.at(l, u))
                    for k in range(5 if UNITS[u][1] < 4 else 1):
                        last = nc.tensor.transpose(in_tiles[:, 16 + k, :], probs[:, u % 2, k * P:(k + 1) * P], ident)
                    last.then_inc(pt_mm.sem, 1)

                def attend(l, u):
                    h, t = UNITS[u]
                    pe.wait_ge(pt_ready.sem, pt_ready.at(l, u + 1))
                    if u >= 2:
                        pe.wait_ge(om_ready.sem, om_ready.at(l, u - 1))
                    tiles = (0, 1, 2, 3, 5) if t < 4 else (4,)
                    for k, vt in enumerate(tiles):
                        last = mm(PS[C * (h % 2):C * (h % 2) + C, 6 + u % 2, 0:P], V[:, vt, h * D_V:(h + 1) * D_V],
                                  probs_t[:, u % 2, k * P:(k + 1) * P], k == 0, k == len(tiles) - 1)
                    last.then_inc(pv_mm.sem, 1)

                n = len(UNITS)
                for u in range(n + 2):
                    if u < n:
                        scores(l, u)
                    if 1 <= u <= n:
                        turn_probs(l, u - 1)
                    if u >= 2:
                        attend(l, u - 2)
                pe.wait_ge(osq_ready.sem, osq_ready.at(l, 1))
                sums(0, ones, [osq[:, k, :] for k in range(4)]).then_inc(ostat_mm.sem, 1)
                pe.wait_ge(mix_lo.sem, mix_lo.at(l, KT))
                hold()
                with pe.Fori(0, N_OUT // 2) as i:
                    for p in range(2):
                        begin(l, 2 * i + (AT_OUT + p))
                        two_tiles(p).then_inc(chunk_done.sem, 1)

                norm(l, 2)
                ffn(l, 1, AT_FFN[1])


def rope_tables():
    n = D_ROPE // 4
    pos = np.stack([np.arange(LAT) // 64, np.arange(LAT) % 64]).astype(np.float32)
    freq = (np.float32(10000.0) ** (-np.arange(n, dtype=np.float32) / n)).astype(np.float32)
    ang = (pos[:, None, None, :] * freq[None, None, :, None]).astype(np.float32)
    ang = np.broadcast_to(ang, (2, 2, n, LAT)).reshape(D_ROPE, LAT)
    out = np.zeros((P, 2 * LAT + P), np.float32)
    turn = out[64:96, 2 * LAT + 64:2 * LAT + 96]
    for a in range(2):
        for f in range(n):
            x1, x2 = a * 2 * n + f, a * 2 * n + n + f
            turn[x2, x1] = -1.0
            turn[x1, x2] = 1.0
    out[64:96, 0:2 * LAT] = np.concatenate([np.cos(ang), np.sin(ang)], 1)
    return out


def fourier_tables():
    def table(n):
        a = 2 * np.pi * (np.outer(np.arange(n), np.arange(n)) % n) / n
        s = 1 / np.sqrt(n * 64.0)
        return np.cos(a) * s, -np.sin(a) * s
    c, s = (m.reshape(4, P, LAT).transpose(1, 0, 2).reshape(P, 4 * LAT) for m in table(LAT))
    cc, ss = table(CTX)
    return np.ascontiguousarray(np.concatenate([c, s, cc, ss], 1).astype(np.float32))


def const_tables():
    pair = np.kron(np.eye(2), np.ones((C, C)))
    s, t = np.arange(P)[:, None] % C, np.arange(C)[None, :]
    masks = [(s == t)] + [(s // (2 * m) == t // (2 * m)) & (s // m != t // m) for m in LEVELS]
    a = 2 * np.pi * (np.outer(np.arange(64), np.arange(64)) % 64) / 64
    chan = [np.kron(np.eye(2), f(a)) for f in (np.cos, np.sin)]
    add = np.zeros((P, 2))
    add[0:4] = np.kron(np.ones((2, 1)), np.eye(2))
    return np.ascontiguousarray(np.concatenate([np.ones((P, P)), pair, np.eye(P), *masks, *chan, add], 1).astype(np.float32))


_OUTS = [("yT", (P, KT, T)), ("ckv_out", (DEPTH, P, KVT, CTX)), ("kr_out", (DEPTH, D_ROPE, CTX)),
         ("state_out", (DEPTH, P, 2, 2, C))]


def kernel(x_prompt, x_sample, cache_ckv, cache_krope, state_hgrn, c, c_ctx, ada_w, ada_b, norm_g, ffn_w_gu,
           ffn_w_down, w_in, hgrn_lb, hgrn_norm_g, mla_q_norm_g, mla_w_q_up, mla_kv_norm_g, mla_w_kv_up,
           mla_qk_norm_g, mla_out_norm_g, fnet_w, fnet_norm_g, w_out):
    import numpy as np
    import concourse.bacc as bacc
    from concourse import mybir as _mybir
    from concourse.bass_utils import run_bass_kernel_spmd

    f = np.float32
    L = DEPTH
    def tiles(a, *lead):
        return np.swapaxes(a.reshape(*a.shape[:-1], -1, P), -1, -2)

    x = np.concatenate([x_sample[0], x_prompt[0]], 0)
    ins = {}
    ins["xT"] = x.reshape(T, KT, P).transpose(2, 1, 0)
    ins["condT"] = np.stack([c[0], c_ctx], -1).reshape(KT, P, 2).transpose(1, 0, 2)
    ada = ada_w.reshape(L, KT, P, N_ADA, 256).transpose(0, 3, 2, 1, 4).reshape(L * N_ADA, P, CHUNK)
    ins["ada_p"] = np.concatenate([ada, np.zeros((2, P, CHUNK), f)], 0)
    pk = [tiles(ada_b), np.concatenate([tiles(norm_g[:, i]) for i in range(3)], -1),
          np.concatenate([hgrn_norm_g, hgrn_norm_g], 1)[:, :, None], tiles(mla_q_norm_g), tiles(mla_kv_norm_g),
          np.concatenate([mla_qk_norm_g.transpose(0, 2, 1), np.zeros((L, P - D_QK, 2), f)], 1),
          tiles(mla_out_norm_g), tiles(fnet_norm_g)]
    ins["params"] = np.concatenate(pk, -1)
    ins["lb"] = hgrn_lb.reshape(L, 2, 2, P).transpose(3, 0, 1, 2).reshape(P, L, 4)
    gu = ffn_w_gu.reshape(L * 2, KT, P, 2, FT, P).transpose(0, 4, 2, 1, 3, 5)
    ins["gu_p"] = gu.reshape(L * 2 * FT, P, CHUNK)
    dn = ffn_w_down.reshape(L * 2, FT, P, KT, P)
    a = FF_PARTS[0]
    for name, part in (("down_a", dn[:, :a]), ("down_b", dn[:, a:])):
        ins[name] = part.transpose(0, 3, 2, 1, 4).reshape(L * 2 * KT, P, -1)
    z = lambda n: np.zeros((L, D_MODEL, n), f)
    cols = np.concatenate([w_in[:, :, :1920], z(64), w_in[:, :, 1920:1952], z(32), w_in[:, :, 1952:]], -1)
    ins["win_p"] = cols.reshape(L, KT, P, N_WIN, 256).transpose(0, 3, 2, 1, 4).reshape(L * N_WIN, P, CHUNK)
    ins["kv_p"] = mla_w_kv_up.reshape(L, KVT, P, 1024).transpose(0, 2, 1, 3).reshape(L, P, CHUNK)
    q = mla_w_q_up.reshape(L, QT_, P, 2, 4, D_QK)
    q = np.concatenate([q, np.zeros((L, QT_, P, 2, 4, P - D_QK), f)], -1)
    ins["q_p"] = q.transpose(0, 3, 2, 1, 4, 5).reshape(L * 2, P, QT_ * 4 * P)
    ins["out_p"] = w_out.reshape(L, KT, P, N_OUT, 256).transpose(0, 3, 2, 1, 4).reshape(L * N_OUT, P, CHUNK)
    fw = np.zeros((L, P, 2, P), f)
    for g in range(4):
        r = slice(64 * (g % 2), 64 * (g % 2) + 64)
        fw[:, r, g // 2, r] = fnet_w[:, g]
    ins["fnet_w"] = fw
    ins["ckvT"] = cache_ckv[0].transpose(0, 2, 1).reshape(L, KVT, P, PAST).transpose(0, 2, 1, 3)
    ins["kropeT"] = cache_krope[0].transpose(0, 2, 1)
    ins["state"] = state_hgrn[0].reshape(L, 2, 2, 2 * 64, 64).transpose(0, 3, 1, 2, 4)
    ins["dft"], ins["consts"], ins["rope"] = fourier_tables(), const_tables(), rope_tables()

    nc = bacc.Bacc("TRN2", target_bir_lowering=False, num_devices=1)
    arrays, args = {}, []
    for name in ("xT", "condT", "ada_p", "params", "lb", "gu_p", "down_a", "down_b", "win_p", "kv_p", "q_p", "out_p",
                 "fnet_w", "ckvT", "kropeT", "state", "dft", "consts", "rope"):
        arr = np.ascontiguousarray(ins[name])
        arrays[f"in_{name}"] = arr
        args.append(nc.dram_tensor(f"in_{name}", arr.shape, _mybir.dt.from_np(arr.dtype), kind="ExternalInput").ap())
    for name, shape in _OUTS:
        args.append(nc.dram_tensor(f"out_{name}", shape, _mybir.dt.float32, kind="ExternalOutput").ap())
    build(nc, *args)
    r = run_bass_kernel_spmd(nc, [arrays], core_ids=[0]).results[0]
    y = np.asarray(r["out_yT"]).transpose(2, 1, 0).reshape(T, D_MODEL)
    ckv = np.asarray(r["out_ckv_out"]).transpose(0, 3, 2, 1).reshape(1, L, CTX, KV_RANK)
    kr = np.asarray(r["out_kr_out"]).transpose(0, 2, 1).reshape(1, L, CTX, D_ROPE)
    st = np.asarray(r["out_state_out"]).transpose(0, 2, 3, 1, 4).reshape(1, L, 2, 4, 64, 64)
    return (np.ascontiguousarray(y[None, LAT:]), np.ascontiguousarray(y[None, :LAT]), np.ascontiguousarray(ckv),
            np.ascontiguousarray(kr), np.ascontiguousarray(st))
```

```python
import numpy as np
import concourse.bass as bass
from concourse import mybir
from contextlib import ExitStack

P = 128
D_MODEL = 1024
KT = D_MODEL // P
LAT, CTX, PAST = 512, 128, 128
T = LAT + CTX
HT = T // 2
KEYS = T + PAST
HK = KEYS // 2
DEPTH = 2
D_FF = 2816
FT = D_FF // P
FF_PARTS = (12, 10)
N_MOD = 9
MT = N_MOD * KT
CHUNK = 2048
N_ADA = MT // 2
ADA_FIRST = 8
PIECES_T, PIECES_V = 8, 6
ADA_LOOPS = {(0, 0): ((1, 6, 7),), (0, 1): ((0, 4, 27), (4, 5, None)),
             (1, 0): ((1, 5, -2), (5, 6, None)), (1, 1): ((0, 5, None),)}
ADA_LOADS = {(0, 0): ((1, 6, (True, True)),), (0, 1): ((0, 3, (True, True)), (3, 4, (True, False)), (4, 5, (False, False))),
             (1, 0): ((1, 4, (True, True)), (4, 5, (True, False)), (5, 6, (False, False))),
             (1, 1): ((0, 5, (False, False)),)}
ADA_COUNT = {(0, 0): -1, (0, 1): 7, (1, 0): 26, (1, 1): 0}
ADA_DOWN = 11
N_WIN = 9
N_QUP = 2
N_OUT = 4
H_MLA, D_NOPE, D_ROPE, D_V = 8, 64, 32, 64
D_QK = D_NOPE + D_ROPE
Q_RANK, KV_RANK = 384, 256
QT_, KVT = Q_RANK // P, KV_RANK // P
EPS = 1e-6
C = 64
NC_LAT, NC_CTX = LAT // C, CTX // C
NCH = NC_LAT + NC_CTX
NU = 2 * NCH
LEVELS = (1, 2, 4, 8, 16, 32)
N_FFN = sum(p + KT for p in FF_PARTS)
PER_LAYER = 2 * N_FFN + N_WIN + 1 + N_QUP + N_OUT
AT_FFN = (0, PER_LAYER - N_FFN)
AT_WIN = N_FFN
AT_OUT = AT_WIN + N_WIN + 1 + N_QUP
U_Q, U_F, U_V, U_GATE, U_CQ, U_CKV, U_KR, U_FN, N_U = 0, 2, 6, 8, 10, 13, 15, 16, 18
PK = {}
_at = 0
for _name, _n in (("norm_g", 3 * KT), ("hgrn_g", 1), ("q_g", QT_), ("kv_g", KVT), ("qk_g", 2),
                  ("mla_g", 4), ("fnet_g", 2)):
    PK[_name] = (_at, _n)
    _at += _n
N_PK = _at


MIX_AT = {6: 0, 0: 2, 2: 4}


class Signal:

    def __init__(self, sem, per, first=0):
        self.sem, self.per, self.first = sem, per, first

    def at(self, layer, k):
        return layer * self.per + (k + self.first)


def build(nc, xT, condT, cond_b, ada_p, ada_first, ada_second, ada_b, params, lb, gu_p, down_a, down_b, win_p, kv_p, q_p,
          out_p, fnet_w, ckvT, kropeT,
          state, dft, consts, level_masks, rope, yT, ckv_out, kr_out, state_out):
    fp32, fp32r, u32 = mybir.dt.float32, mybir.dt.float32r, mybir.dt.uint32
    ALU, ACT, AX = mybir.AluOpType, mybir.ActivationFunctionType, mybir.AxisListType

    ctx = ExitStack()
    with ctx:
        def sem(name):
            return ctx.enter_context(nc.semaphore(name))

        def signal(name, per, first=0):
            return Signal(sem(name), per, first)

        def sb(name, shape, dt=fp32):
            return ctx.enter_context(nc.sbuf_tensor(name, shape, dt))

        X = sb("X", [P, KT, T])
        H_hi = sb("H_hi", [P, KT, T], fp32r)
        H_lo = sb("H_lo", [P, KT, T], fp32r)
        raw = [sb(f"raw{i}", [P, CHUNK]) for i in range(2)]
        W_hi = [sb(f"W_hi{i}", [P, CHUNK], fp32r) for i in range(2)]
        W_lo = [sb(f"W_lo{i}", [P, CHUNK], fp32r) for i in range(2)]
        ada_bt = sb("ada_bt", [P, 2 * (DEPTH * N_ADA + ADA_FIRST), 1])
        konst = sb("konst", [P, 5 * P])
        ones, pair_ones, ident = (konst[:, i * P:(i + 1) * P] for i in range(3))
        chan = konst[:, 3 * P:5 * P]
        par = sb("par", [P, N_PK])
        mod = sb("mod", [P, MT, 2])
        up_by = sb("up_by", [P, 3, KT, 2])
        gates = sb("gates", [P, 3, KT, 2])
        cond = sb("cond", [P, KT, 2])
        cond_f = sb("cond_f", [P, KT, 2])
        ada_sum = sb("ada_sum", [P, 2, 2])
        lbt = sb("lbt", [P, 2, 4])
        lbs = sb("lbs", [P, 2, 4])
        rest = sb("rest", [P, 2, 4])
        lb_l = sb("lb_l", [P, 2, 4])
        eps = sb("eps", [P, 1])
        qk_g = sb("qk_g", [P, 2])
        fw_t = sb("fw_t", [P, 2, P])
        D64 = sb("D64", [P, 2, 2, NCH])
        ckvc = sb("ckvc", [P, KVT, PAST])
        krc = sb("krc", [P, PAST])
        fin_s = sb("fin_s", [P, 2, 2, C])
        nmax = sb("nmax", [P, 8])
        rsum = sb("rsum", [P, 8])
        rinv = sb("rinv", [P, 8])

        R0 = (nc.sbuf_base + 31) // 32 * 32
        ROOM = nc.sbuf_usable_end - R0
        TB, KB = 4 * T, 4 * KEYS

        def at(name, offset, shape, dt=fp32):
            size = 4
            for n in shape[1:]:
                size *= n
            assert offset + size <= ROOM, (name, offset + size, ROOM)
            return nc.alloc_sbuf_tensor_at(name, shape, dt, offset=R0 + offset)

        first_raw = at("first_raw", 0, [P, PIECES_T + PIECES_V, D_MODEL])
        ada_raw = at("ada_raw", 28 * TB, [P, 2, D_MODEL])
        cond_bc = at("cond_bc", 28 * TB + 4 * CHUNK, [P, 2, D_MODEL])
        unused = at("unused", 28 * TB + 8 * CHUNK, [P, D_MODEL])
        rsq = at("rsq", 8 * TB, [P, T])
        norm_t = at("norm_t", 9 * TB, [P, KT, T])
        F_hi = at("F_hi", 0, [P, FF_PARTS[0], T], fp32r)
        F_lo = at("F_lo", 12 * TB, [P, FF_PARTS[0], T], fp32r)
        silu_t = at("silu_t", 24 * TB, [P, 2, T])
        ffn_t = at("ffn_t", 26 * TB, [P, 2, T])
        sq2, sum_x = silu_t, ffn_t[:, 0, :]
        U = at("U", 0, [P, N_U, T])
        E0 = N_U * TB
        dft_t = at("dft_t", E0, [P, 8 * LAT + 2 * P])
        Y = at("Y", E0 + 17408, [P, 5, 4 * P])
        spec = at("spec", E0 + 17408 + 4 * TB, [P, 2, T])
        fsq = at("fsq", E0, [P, 2, T])
        frs = at("frs", E0 + 2 * TB, [P, T])
        fmix = at("fmix", E0 + 10 * TB, [P, 2, T])
        KP = at("KP", E0, [P, 2, 2, T])
        QP = at("QP", E0 + 4 * TB, [P, 2, 2, T])
        A = at("A", E0 + 8 * TB, [P, NU, C])
        Vtok = at("Vtok", E0 + 10 * TB, [P, NU, C])
        D_a = U[:, U_F:U_F + 4, :].rearrange("p (d a) t -> p d (a t)", d=2)
        D_b = at("D_b", E0 + 12 * TB, [P, 2, T])
        S = at("S", E0 + 12 * TB, [P, 2, 2, NCH, C])
        masks = at("masks", E0 + 12 * TB + 16 * NCH * C, [P, 7, C])
        rope_t = at("rope_t", E0 + 12 * TB + 16 * NCH * C + 28 * C, [P, 2 * LAT + P])
        cos, sin = rope_t[64:96, 0:LAT], rope_t[64:96, LAT:2 * LAT]
        turn = rope_t[0:D_QK, 2 * LAT:2 * LAT + P]
        Ktok = at("Ktok", U_F * TB, [P, 2 * NU, C])
        Kc = [at(f"Kc{i}", t * TB, [P, 2 * T]) for i, t in enumerate((U_V, U_FN))]
        hsq = at("hsq", E0, [P, 2 * T])
        hrs = at("hrs", E0 + 2 * TB, [P, 2 * T])
        hmix = at("hmix", E0 + 4 * TB + 4 * KEYS * 4, [P, 2, T])
        csq_q = at("csq_q", E0 + 13 * TB, [P, QT_, T])
        csq_kv = at("csq_kv", E0 + 8 * TB, [P, KVT, T])
        crs = at("crs", E0 + 14 * TB, [P, 2, T])
        cq_hi, cq_lo = H_hi[:, 2:2 + QT_, :], H_lo[:, 2:2 + QT_, :]
        ck_hi = at("ck_hi", E0 + 4 * TB, [P, KVT, KEYS], fp32r)
        ck_lo = at("ck_lo", E0 + 4 * TB + 2 * KB, [P, KVT, KEYS], fp32r)
        K_t = at("K_t", 0, [D_QK, H_MLA, KEYS])
        V = at("V", 8 * KB, [P, 6, H_MLA * D_V])
        ksq = at("ksq", 12 * KB, [D_QK, 2, KEYS])
        E1 = E0 + 6 * TB + 4 * KB
        kraw = at("kraw", E1, [D_QK, 2, KEYS])
        krs = at("krs", E1 + 2 * KB, [D_QK, 2, KEYS])
        Q_t = at("Q_t", 12 * KB, [D_QK, H_MLA, T])
        qsq = at("qsq", E1, [D_QK, 2, T])
        qraw = at("qraw", E1 + 2 * TB, [D_QK, 2, T])
        qrs = at("qrs", E1 + 4 * TB, [D_QK, 1, T])
        E2 = 12 * KB + 8 * TB
        probs = at("probs", E2, [P, 2, T])
        probs_t = at("probs_t", E2 + 2 * TB, [P, 2, T])
        O_m = at("O_m", E2 + 4 * TB, [P, 4, T])
        osq = at("osq", 0, [P, 4, T])
        ors = at("ors", 4 * TB, [P, T])

        PS = ctx.enter_context(nc.psum_tensor("PS", [P, 8, 512], fp32))
        flat = PS[:, :, :].rearrange("p b n -> p (b n)")
        in_tiles = flat.rearrange("p (u c) -> p u c", c=P)

        landed = [signal(f"weights_landed{i}", 8 * PER_LAYER) for i in range(2)]
        hi_ready = signal("weights_hi_ready", PER_LAYER)
        split_ready = signal("weights_split", PER_LAYER)
        chunk_done = signal("chunk_multiplied", PER_LAYER, 2)
        emptied = signal("chunk_emptied", PER_LAYER, 2)
        const_landed = sem("const_landed")
        setup = signal("setup_step", 0)
        par_landed = signal("par_landed", 64)
        first_landed = [sem(f"first_ada_landed{i}") for i in range(PIECES_T + PIECES_V + 1)]
        first_cond_landed = sem("first_cond_landed")
        first_cond = sem("first_cond_silu")
        first_sum = sem("first_ada_summed")
        cond_landed = signal("cond_landed", 16)
        cond_ready = signal("cond_silu", 1)
        tables_landed = signal("tables_landed", 32)
        ada_landed = signal("ada_landed", 16 * N_ADA)
        ada_used = signal("ada_used", N_ADA + 1, 1)
        mod_ready = signal("mod_ready", 3)
        sq_ready = signal("x_squares", 3 * KT, KT)
        sq_used = signal("x_squares_added", 3 * KT, KT)
        sum_ready = signal("x_squares_summed", 3)
        stat_mm = signal("norm_sums", 3)
        rs_ready = signal("norm_rsqrt", 3)
        scaled = signal("norm_scaled", 3 * KT)
        h_hi = signal("h_hi_ready", 3 * KT)
        h_lo = signal("h_lo_ready", 3 * KT)
        gate_ready = signal("ffn_silu", 2 * FT)
        f_hi = signal("ffn_hi", 2 * FT)
        f_lo = signal("ffn_lo", 2 * FT, 2)
        dft_landed = signal("dft_landed", 16)
        y_mm = signal("fourier_rows", 5)
        y_ready = signal("fourier_rows_copied", 5)
        spec_mm = signal("fourier_spec", 2)
        spec_ready = signal("fourier_spec_copied", 2)
        fn_mm = signal("fourier_out", 2)
        fsq_ready = signal("fourier_squares", 1)
        fstat_mm = signal("fourier_sums", 1)
        frs_ready = signal("fourier_rsqrt", 1)
        mixed = signal("mix_ready", KT)
        mix_hi = signal("mix_hi_ready", KT)
        mix_lo = signal("mix_lo_ready", KT)
        gates_ready = signal("hgrn_gates", 2)
        vt_mm = signal("hgrn_v_turned", 1)
        v_tok = signal("hgrn_v_ready", 1)
        lev_ready = signal("level_ready", 2 + 2 * len(LEVELS))
        lev_mm = signal("level_scores", 2 + 2 * len(LEVELS))
        merged = signal("level_merged", 1 + len(LEVELS))
        kt_mm = signal("hgrn_k_turned", 1)
        k_tok = signal("hgrn_k_ready", 1)
        kv_mm = signal("hgrn_kv", 1)
        s0_landed = signal("state_landed", 32)
        s_ready = signal("states_ready", 1)
        o_mm = signal("hgrn_out", 1)
        hsq_ready = signal("hgrn_squares", 1)
        hstat_mm = signal("hgrn_sums", 1)
        hrs_ready = signal("hgrn_rsqrt", 1)
        csq_ready = signal("latent_squares", 1)
        cstat_mm = signal("latent_sums", 1)
        crs_ready = signal("latent_rsqrt", 1)
        c_normed = signal("latent_normed", 1)
        cq_hi_ready = signal("query_latent_hi", 1)
        cq_lo_ready = signal("query_latent_lo", 1)
        ck_hi_ready = signal("key_latent_hi", 1)
        ck_lo_ready = signal("key_latent_lo", 1)
        stored = signal("cache_stored", 32)
        state_stored = signal("state_stored", 16)
        q_ready = signal("queries_ready", 1)
        heads = {}
        for kind in "kq":
            for what in ("proj", "copied", "squares", "sums", "rsqrt", "normed", "turned_mm", "turned"):
                heads[kind, what] = signal(f"{kind}_{what}", H_MLA)
        v_mm = signal("v_rows", 6)
        v_ready = signal("v_rows_copied", 6)
        UNITS = [(h, t) for h in range(H_MLA) for t in range(5)]
        sc_mm = signal("scores", len(UNITS))
        max_ready = signal("scores_max", len(UNITS))
        exp_ready = signal("probs_exp", len(UNITS))
        p_ready = signal("probs_scaled", len(UNITS))
        pt_mm = signal("probs_turned", len(UNITS))
        pt_ready = signal("probs_t_ready", len(UNITS))
        pv_mm = signal("attn_out", len(UNITS))
        om_ready = signal("attn_out_copied", len(UNITS))
        osq_ready = signal("mla_squares", 1)
        ostat_mm = signal("mla_sums", 1)
        ors_ready = signal("mla_rsqrt", 1)
        y_stored = sem("y_stored")
        x_landed = sem("x_landed")
        wait_passed = sem("wait_passed")

        block = ctx.enter_context(nc.Block())

        def col(name, k=0):
            return par[:, PK[name][0] + k:PK[name][0] + k + 1]

        def halves(bank, n=HT, rows=slice(0, P)):
            return PS[rows, bank:bank + 2, 0:n]

        def two(ap, n=HT):
            return ap.rearrange("p (j n) -> p j n", n=n)

        def flip(t, first, m):
            f = t[:, 0:1, 0:1, first * m:first * m + 1]
            step = 2 * T + (m if first == 0 else -m)
            return bass.AP(f.tensor, f.offset, [list(f.ap[0]), [step, 2], [2 * m, T // m], [1, m]])

        def flip_pair(t, first, m, a):
            f = t[:, 0:1, a:a + 1, first * m:first * m + 1]
            step = 2 * T + (m if first == 0 else -m)
            return bass.AP(f.tensor, f.offset, [list(f.ap[0]), [step, 2], [2 * m, T // (2 * m)], [1, m]])

        def each(t, first, n, m, at_=0):
            f = t[:, 0:1, at_ + first:at_ + first + 1]
            step = t.shape[2] + (1 if first == 0 else -1)
            return bass.AP(f.tensor, f.offset, [list(f.ap[0]), [step, 2], [2, n], [0, m]])

        def pick(t, m, u, rows):
            f = t[rows, 1:2, u // NCH:u // NCH + 1, u % NCH * C:u % NCH * C + 1]
            return bass.AP(f.tensor, f.offset, [list(f.ap[0]), [2 * m, C // (2 * m)], [m - 2 * T, 2], [1, m]])

        def merge(t, m):
            f = t[:, 0:1]
            return bass.AP(f.tensor, f.offset, [list(f.ap[0]), [m, 2], [2 * m, T // m], [1, m]])

        GROUPS = ((0, 0, HT, 0), (1, HT, LAT, 0), (1, LAT, T, 1))

        def alternate(units):
            banks = sorted({u // 8 for u in units})
            order = []
            n = len(banks)
            for i in range(n):
                for r, b in ((0, banks[i]), (1, banks[(i + 1) % n])):
                    order.append((r, [u for u in units if u // 8 == b]))
            return order

        @block.sync
        def _(sp):
            def load(l, c, p, src, size):
                sp.wait_ge(split_ready.sem, split_ready.at(l, c - 1))
                sp.dma_start(raw[p][:, 0:size], src).then_inc(landed[p].sem, 16)

            for n in range(PIECES_T):
                sp.dma_start(first_raw[:, n, :], ada_first[n]).then_inc(first_landed[n], 16)
                if n < PIECES_V:
                    sp.dma_start(first_raw[:, PIECES_T + n, :], ada_second[n]).then_inc(first_landed[PIECES_T + n], 16)
            sp.dma_start(ada_raw[:, :, :].rearrange("p k c -> p (k c)"), ada_p[0])\
              .then_inc(first_landed[-1], 16)
            for p in range(2):
                sp.dma_start(raw[p][:, :], gu_p[p]).then_inc(landed[p].sem, 16)

            with sp.Fori(0, DEPTH) as l:
                def load_ffn(f, c):
                    for part, (size, down) in enumerate(zip(FF_PARTS, (down_a, down_b))):
                        q0 = FF_PARTS[0] * part
                        with sp.Fori(1 - part, size // 2) as i:
                            for p in range(2):
                                load(l, 2 * i + (c + p), p, gu_p[(2 * l + f) * FT + 2 * i + (q0 + p)], CHUNK)
                        c += size
                        with sp.Fori(0, KT // 2) as i:
                            for p in range(2):
                                load(l, 2 * i + (c + p), p, down[(2 * l + f) * KT + 2 * i + p], size * P)
                        c += KT

                load_ffn(0, AT_FFN[0])
                with sp.Fori(0, 4) as i:
                    for p in range(2):
                        load(l, 2 * i + (AT_WIN + p), p, win_p[l * N_WIN + 2 * i + p], CHUNK)
                load(l, AT_WIN + 8, 0, win_p[l * N_WIN + 8], CHUNK)
                load(l, AT_WIN + 9, 1, kv_p[l], CHUNK)
                for p in range(2):
                    load(l, AT_WIN + 10 + p, p, q_p[2 * l + p], QT_ * 4 * P)
                with sp.Fori(0, N_OUT // 2) as i:
                    for p in range(2):
                        load(l, 2 * i + (AT_OUT + p), p, out_p[l * N_OUT + 2 * i + p], CHUNK)
                for p in range(2):
                    load(l, AT_FFN[1] + p, p, gu_p[(2 * l + 1) * FT + p], CHUNK)
                load_ffn(1, AT_FFN[1])
                for p in range(2):
                    load(l, PER_LAYER + p, p, gu_p[(l + 1) * (2 * FT) + p], CHUNK)
            for a, b in ((0, KT - 2), (KT - 2, KT)):
                sp.wait_ge(emptied.sem, emptied.at(DEPTH, b - KT))
                sp.dma_start(yT[:, a:b, :], X[:, a:b, :]).then_inc(y_stored, 16)
            sp.wait_ge(y_stored, 32)
            for p in range(2):
                sp.wait_ge(landed[p].sem, 8 * PER_LAYER * DEPTH + 16)

        @block.gpsimd
        def _(pool):
            def load_ada(l, f, n):
                pool.wait_ge(ada_used.sem, ada_used.at(l, n + f))
                pool.dma_start(ada_raw[:, :, :].rearrange("p k c -> p (k c)"), ada_p[l * N_ADA + n + 1])\
                    .then_inc(ada_landed.sem, 16)

            def low(l, q, slot, p):
                pool.wait_ge(f_hi.sem, f_hi.at(l, q + 1))
                pool.tensor_tensor(F_lo[:, bass.ds(slot, 1), :], ffn_t[:, p:p + 1, :],
                                   F_hi[:, bass.ds(slot, 1), :].bitcast(fp32), ALU.subtract).then_inc(f_lo.sem, 1)

            with pool.Fori(0, DEPTH) as l:
                for f in range(2):
                    load_ada(l, f, ADA_COUNT[f, 0] + 1)
                    if f == 1:
                        pool.dma_start(cond_bc[:, :, :], cond_b).then_inc(cond_landed.sem, 16)
                    low(l, f * FT, 0, 0)
                    load_ada(l, f, ADA_COUNT[f, 0] + 2)
                    low(l, f * FT + 1, 1, 1)
                    for part in range(2):
                        q0 = FF_PARTS[0] * part
                        for a, b, loads in ADA_LOADS[f, part]:
                            with pool.Fori(a, b) as i:
                                for p in range(2):
                                    if loads[p]:
                                        load_ada(l, f, 2 * i + (q0 + p + ADA_COUNT[f, part] + 1))
                                    low(l, 2 * i + (f * FT + q0 + p), 2 * i + p, p)
                        if (f, part) == (0, 0):
                            with pool.Fori(0, KT) as i:
                                load_ada(l, f, i + (ADA_DOWN + 1))
                    if f == 0:
                        pool.wait_ge(crs_ready.sem, crs_ready.at(l, 1))
                        for k in range(QT_ + KVT):
                            pool.tensor_tensor(U[:, U_CQ + k, :], U[:, U_CQ + k, :], crs[:, k // QT_, :], ALU.mult)
                        pool.drain()
                        for k in range(QT_ + KVT):
                            gain = col("q_g", k) if k < QT_ else col("kv_g", k - QT_)
                            pool.tensor_scalar(U[:, U_CQ + k, :], U[:, U_CQ + k, :], gain, None, ALU.mult)
                        pool.drain().then_inc(c_normed.sem, 1)
                        pool.wait_ge(cq_hi_ready.sem, cq_hi_ready.at(l, 1))
                        pool.tensor_tensor(cq_lo, U[:, U_CQ:U_CQ + QT_, :], cq_hi.bitcast(fp32),
                                           ALU.subtract).then_inc(cq_lo_ready.sem, 1)
            pool.wait_ge(f_lo.sem, f_lo.at(DEPTH, 0))

        @block.scalar
        def _(act):
            def split_hi(l, c, p):
                act.wait_ge(landed[p].sem, landed[p].at(l, 8 * (c - p) + 16))
                act.wait_ge(chunk_done.sem, chunk_done.at(l, c - 1))
                act.activation(W_hi[p][:, :], raw[p][:, :], ACT.Copy).then_inc(hi_ready.sem, 1)

            def rsqrt(out, src, width):
                act.activation(out, src, ACT.Ln, bias=eps[0:out.shape[0], :], scale=1.0 / width)
                act.drain()
                return act.activation(out, out, ACT.Exp, scale=-0.5)

            def log_exp_tables():
                act.preload_act_table_set("natural_log_exp_and_others")

            act.sem_inc(f_lo.sem, 2)
            act.dma_start(cond[:, :, :], condT).then_inc(first_cond_landed, 16)
            act.dma_start(cond_bc[:, :, :], cond_b).then_inc(first_cond_landed, 16)
            for dst, src in ((lbt, lb), (konst, consts), (ada_bt, ada_b)):
                act.dma_start(dst[tuple(slice(None) for _ in dst.shape)], src).then_inc(const_landed, 16)
            act.dma_start(X[:, :, :], xT).then_inc(x_landed, 16)
            act.wait_ge(first_cond_landed, 32)
            act.activation(cond_f[:, :, :], cond[:, :, :], ACT.Silu).then_inc(first_cond, 1)
            act.activation(cond_bc[:, :, :], cond_bc[:, :, :], ACT.Silu).then_inc(first_cond, 1)
            act.wait_ge(setup.sem, 1)
            act.activation(lbs[:, :, :], lbt[:, :, :], ACT.Exp).then_inc(setup.sem, 1)
            act.wait_ge(x_landed, 16)
            for k in range(KT):
                if k >= 2:
                    act.wait_ge(sq_used.sem, k - 1)
                act.activation(sq2[:, k % 2, :], X[:, k, :], ACT.Square).then_inc(sq_ready.sem, 1)
            act.wait_ge(landed[0].sem, 16)
            act.activation(W_hi[0][:, :], raw[0][:, :], ACT.Copy).then_inc(hi_ready.sem, 1)

            def square_x(l, j, c, k, p):
                act.wait_ge(emptied.sem, emptied.at(l, c))
                act.wait_ge(sq_used.sem, sq_used.at(l, k + (j * KT - 1)))
                act.activation(sq2[:, p, :], X[:, bass.ds(k, 1), :].rearrange("p o t -> p (o t)"),
                               ACT.Square).then_inc(sq_ready.sem, 1)

            def norm(l, j):
                log_exp_tables()
                act.wait_ge(stat_mm.sem, stat_mm.at(l, j + 1))
                rsqrt(two(rsq[:, :]), halves(0), D_MODEL).then_inc(rs_ready.sem, 1)
                act.wait_ge(mod_ready.sem, mod_ready.at(l, j + 1))
                for k in range(KT):
                    act.wait_ge(scaled.sem, scaled.at(l, j * KT + k + 1))
                    for g, (a, b) in enumerate(((0, LAT), (LAT, T))):
                        done = act.activation(H_hi[:, k, a:b], norm_t[:, k, a:b], ACT.Identity,
                                              bias=mod[:, 3 * j * KT + k, g:g + 1])
                    done.then_inc(h_hi.sem, 1)

            def ffn(l, f, c):
                done = 0
                for part in FF_PARTS:
                    with act.Fori(0, part // 2) as i:
                        for p in range(2):
                            split_hi(l, 2 * i + (c + p + 1), 1 - p)
                            act.wait_ge(chunk_done.sem, chunk_done.at(l, 2 * i + (c + p + 1)))
                            act.activation(two(silu_t[:, p, :]), halves(4 * p), ACT.Silu).then_inc(gate_ready.sem, 1)
                            act.wait_ge(emptied.sem, emptied.at(l, 2 * i + (c + p + 1)))
                            act.activation(F_hi[:, bass.ds(2 * i + p, 1), :], ffn_t[:, p:p + 1, :],
                                           ACT.Copy).then_inc(f_hi.sem, 1)
                    done += part
                    c += part
                    with act.Fori(0, KT // 2) as i:
                        for p in range(2):
                            split_hi(l, 2 * i + (c + p + 1), 1 - p)
                            if done == FT:
                                square_x(l, 2 * f, 2 * i + (c + p + 1), 2 * i + p, p)
                    c += KT

            def to_hi(l, src, t0, n):
                for k in range(n):
                    act.wait_ge(mixed.sem, mixed.at(l, MIX_AT[t0] + k + 1))
                    act.activation(H_hi[:, t0 + k, :], src[:, k, :], ACT.Copy).then_inc(mix_hi.sem, 1)

            with act.Fori(0, DEPTH) as l:
                act.wait_ge(emptied.sem, emptied.at(l, 0))
                act.dma_start(par[:, :], params[l]).then_inc(par_landed.sem, 16)
                act.dma_start(fw_t[:, :, :], fnet_w[l]).then_inc(par_landed.sem, 16)
                act.dma_start(ckvc[:, :, :], ckvT[l]).then_inc(par_landed.sem, 16)
                act.dma_start(krc[64:96, :], kropeT[l]).then_inc(par_landed.sem, 16)

                norm(l, 0)
                ffn(l, 0, AT_FFN[0])

                norm(l, 1)
                act.wait_ge(h_lo.sem, h_lo.at(l, 2 * KT))
                act.dma_start(dft_t[:, :], dft).then_inc(dft_landed.sem, 16)
                act.dma_start(masks[:, :, :], level_masks).then_inc(tables_landed.sem, 16)
                act.dma_start(rope_t[:, :], rope).then_inc(tables_landed.sem, 16)

                def empty_u(l, c, p, t):
                    act.wait_ge(chunk_done.sem, chunk_done.at(l, c + 1))
                    act.activation(U[:, bass.ds(t, 1), :].rearrange("p o (j n) -> p (o j) n", n=HT), halves(4 * p), ACT.Copy)
                    act.activation(U[:, bass.ds(t + 1, 1), :].rearrange("p o (j n) -> p (o j) n", n=HT), halves(4 * p + 2),
                                   ACT.Copy).then_inc(emptied.sem, 1)

                with act.Fori(0, 4) as i:
                    for p in range(2):
                        split_hi(l, 2 * i + (AT_WIN + p + 1), 1 - p)
                        empty_u(l, 2 * i + (AT_WIN + p), p, 4 * i + 2 * p)
                split_hi(l, AT_WIN + 9, 1)
                empty_u(l, AT_WIN + 8, 0, U_FN)
                split_hi(l, AT_WIN + 10, 0)

                for t in (U_Q, U_GATE):
                    act.activation(U[:, t:t + 2, :], U[:, t:t + 2, :], ACT.Silu)
                act.activation(csq_q[:, :, :], U[:, U_CQ:U_CQ + QT_, :], ACT.Square)

                for g in range(2):
                    act.wait_ge(spec_mm.sem, spec_mm.at(l, g + 1))
                    act.activation(spec[:, g, 0:LAT], PS[:, 5 + g, :], ACT.Copy)
                    act.activation(spec[:, g, LAT:T], PS[:, 7, g * P:(g + 1) * P], ACT.Copy).then_inc(spec_ready.sem, 1)
                act.activation(csq_kv[:, :, :], U[:, U_CKV:U_CKV + KVT, :], ACT.Square).then_inc(csq_ready.sem, 1)
                for g in range(2):
                    act.wait_ge(fn_mm.sem, fn_mm.at(l, g + 1))
                    sq = act.activation(two(fsq[:, g, :]), halves(2 * g), ACT.Square)
                sq.then_inc(fsq_ready.sem, 1)
                log_exp_tables()
                act.wait_ge(fstat_mm.sem, fstat_mm.at(l, 1))
                rsqrt(two(frs[:, :]), halves(4), 2 * P).then_inc(frs_ready.sem, 1)
                to_hi(l, fmix, 6, 2)

                act.activation(KP[:, :, :, :].rearrange("p d a t -> p (d a) t"), U[:, U_F:U_F + 4, :], ACT.Sigmoid,
                               scale=-1.0).then_inc(gates_ready.sem, 1)
                act.drain()
                act.activation(U[:, U_F:U_F + 4, :], U[:, U_F:U_F + 4, :], ACT.Sigmoid).then_inc(gates_ready.sem, 1)
                act.wait_ge(vt_mm.sem, vt_mm.at(l, 1))
                act.wait_ge(mix_lo.sem, mix_lo.at(l, 2))
                act.activation(Vtok[:, :, :].rearrange("p u v -> p (u v)"), flat[:, 0:NU * C],
                               ACT.Copy).then_inc(v_tok.sem, 1)
                log_exp_tables()
                act.wait_ge(cstat_mm.sem, cstat_mm.at(l, 1))
                rsqrt(two(crs[:, 0, :]), halves(6), Q_RANK)
                rsqrt(two(crs[:, 1, :]), halves(4), KV_RANK).then_inc(crs_ready.sem, 1)
                act.wait_ge(c_normed.sem, c_normed.at(l, 1))
                act.activation(cq_hi, U[:, U_CQ:U_CQ + QT_, :], ACT.Copy).then_inc(cq_hi_ready.sem, 1)
                act.dma_start(ckv_out[l], U[:, U_CKV:U_CKV + KVT, LAT:T]).then_inc(stored.sem, 16)
                act.dma_start(kr_out[l], U[64:96, U_KR, LAT:T]).then_inc(stored.sem, 16)
                act.wait_ge(lev_ready.sem, lev_ready.at(l, 2 + 2 * len(LEVELS)))
                act.dma_start(S[:, 0, :, 0, :], state[l, :, 0]).then_inc(s0_landed.sem, 16)
                act.dma_start(S[:, 1, :, NC_LAT - 1, :], state[l, :, 1]).then_inc(s0_landed.sem, 16)
                act.wait_ge(kt_mm.sem, kt_mm.at(l, 1))
                act.activation(Ktok[:, :, :].rearrange("p u v -> p (u v)"), flat[:, 0:2 * NU * C],
                               ACT.Copy).then_inc(k_tok.sem, 1)
                act.wait_ge(o_mm.sem, o_mm.at(l, 1))
                act.activation(hsq[:, :], flat[:, 5 * 512:5 * 512 + 2 * T], ACT.Square).then_inc(hsq_ready.sem, 1)
                act.activation(ck_hi[:, :, 0:T], U[:, U_CKV:U_CKV + KVT, :], ACT.Copy)
                act.activation(ck_hi[:, :, T:KEYS], ckvc[:, :, :], ACT.Copy).then_inc(ck_hi_ready.sem, 1)
                act.wait_ge(hstat_mm.sem, hstat_mm.at(l, 1))
                rsqrt(hrs[:, :], flat[:, 0:2 * T], C).then_inc(hrs_ready.sem, 1)
                to_hi(l, hmix, 0, 2)

                act.dma_start(state_out[l], fin_s[:, :, :, :]).then_inc(state_stored.sem, 16)

                act.wait_ge(stored.sem, stored.at(l, 32))
                act.wait_ge(ck_lo_ready.sem, ck_lo_ready.at(l, 1))

                def squares(l, kind, h):
                    sg = {what: heads[kind, what] for what in ("copied", "squares", "proj")}
                    if kind == "k":
                        act.wait_ge(sg["copied"].sem, sg["copied"].at(l, h + 1))
                        act.activation(ksq[:, h % 2, :], kraw[:, h % 2, :], ACT.Square).then_inc(sg["squares"].sem, 1)
                    else:
                        act.wait_ge(sg["proj"].sem, sg["proj"].at(l, h + 1))
                        src = halves(2 * (h % 2), rows=slice(0, D_QK))
                        if h >= 2:
                            act.wait_ge(heads["q", "normed"].sem, heads["q", "normed"].at(l, h - 1))
                        act.activation(two(qraw[:, h % 2, :]), src, ACT.Copy).then_inc(sg["copied"].sem, 1)
                        act.activation(two(qsq[:, h % 2, :]), src, ACT.Square).then_inc(sg["squares"].sem, 1)

                def head_rsqrt(l, kind, h):
                    n = HK if kind == "k" else HT
                    out = krs[:, h % 2, :] if kind == "k" else qrs[:, 0, :]
                    act.wait_ge(heads[kind, "sums"].sem, heads[kind, "sums"].at(l, h + 1))
                    before = h - 1 if kind == "k" else h
                    if before >= 1:
                        act.wait_ge(heads[kind, "normed"].sem, heads[kind, "normed"].at(l, before))
                    rsqrt(two(out, n), halves(4, n, slice(0, D_QK)), D_QK).then_inc(heads[kind, "rsqrt"].sem, 1)

                for h in range(H_MLA + 1):
                    if h < H_MLA:
                        squares(l, "k", h)
                    if h >= 1:
                        head_rsqrt(l, "k", h - 1)
                split_hi(l, AT_WIN + 11, 1)
                act.wait_ge(state_stored.sem, state_stored.at(l, 16))
                act.wait_ge(emptied.sem, emptied.at(l, AT_WIN + 10))
                for h in range(H_MLA + 1):
                    if h < H_MLA:
                        squares(l, "q", h)
                    if h >= 1:
                        head_rsqrt(l, "q", h - 1)
                    if h == 5:
                        split_hi(l, AT_OUT, 0)

                def exp(l, u):
                    w = T if UNITS[u][1] < 4 else CTX
                    act.wait_ge(max_ready.sem, max_ready.at(l, u + 1))
                    if u >= 2:
                        act.wait_ge(pt_mm.sem, pt_mm.at(l, u - 1))
                    act.activation(probs[:, u % 2, 0:w], flat[:, 1024 * (u % 2):1024 * (u % 2) + w], ACT.Exp,
                                   bias=nmax[:, u % 8:u % 8 + 1],
                                   accum_out=rsum[:, u % 8:u % 8 + 1]).then_inc(exp_ready.sem, 1)

                def copy_pt(l, u):
                    w = T if UNITS[u][1] < 4 else CTX
                    act.wait_ge(pt_mm.sem, pt_mm.at(l, u + 1))
                    if u >= 2:
                        act.wait_ge(pv_mm.sem, pv_mm.at(l, u - 1))
                    act.activation(probs_t[:, u % 2, 0:w], flat[:, 2048:2048 + w], ACT.Copy).then_inc(pt_ready.sem, 1)

                for u in range(len(UNITS) + 1):
                    if u >= 1:
                        copy_pt(l, u - 1)
                    if u < len(UNITS):
                        exp(l, u)
                act.wait_ge(om_ready.sem, om_ready.at(l, len(UNITS)))
                act.activation(osq[:, :, :], O_m[:, :, :], ACT.Square).then_inc(osq_ready.sem, 1)
                act.wait_ge(ostat_mm.sem, ostat_mm.at(l, 1))
                rsqrt(two(ors[:, :]), halves(4), H_MLA * D_V).then_inc(ors_ready.sem, 1)
                to_hi(l, O_m, 2, 4)
                with act.Fori(0, N_OUT // 2) as i:
                    for p in range(2):
                        split_hi(l, 2 * i + (AT_OUT + p + 1), 1 - p)
                        for t in range(2):
                            square_x(l, 1, 2 * i + (AT_OUT + p + 1), 4 * i + (2 * p + t), t)

                norm(l, 2)
                act.wait_ge(cond_landed.sem, cond_landed.at(l, 16))
                act.activation(cond_bc[:, :, :], cond_bc[:, :, :], ACT.Silu).then_inc(cond_ready.sem, 1)
                ffn(l, 1, AT_FFN[1])

        @block.vector
        def _(dve):
            def split_lo(l, c, p):
                dve.wait_ge(hi_ready.sem, hi_ready.at(l, c + 1))
                dve.tensor_tensor(W_lo[p][:, :], raw[p][:, :], W_hi[p][:, :].bitcast(fp32),
                                  ALU.subtract).then_inc(split_ready.sem, 1)

            dve.sem_inc(chunk_done.sem, 2)
            dve.sem_inc(emptied.sem, 2)
            dve.memset(eps[:, :], EPS)
            dve.wait_ge(const_landed, 48)
            dve.tensor_tensor(rest[:, 0, :], lbt[:, 0, :], lbt[:, 1, :], ALU.max)
            dve.drain()
            for i in range(2):
                done = dve.tensor_tensor(lbt[:, i, :], lbt[:, i, :], rest[:, 0, :], ALU.subtract)
            done.then_inc(setup.sem, 1)
            dve.wait_ge(setup.sem, 2)
            dve.tensor_tensor(lbt[:, 0, :], lbs[:, 0, :], lbs[:, 1, :], ALU.add)
            dve.drain()
            dve.reciprocal(lbt[:, 0, :], lbt[:, 0, :])
            dve.drain()
            dve.tensor_tensor(rest[:, 1, :], lbs[:, 0, :], lbt[:, 0, :], ALU.mult)
            dve.tensor_tensor(lbt[:, 1, :], lbs[:, 1, :], lbt[:, 0, :], ALU.mult)
            dve.memset(rest[:, 0, :], 1.0)
            dve.drain()
            dve.tensor_copy(lbs[:, 1, :], lbt[:, 1, :])
            dve.memset(lbs[:, 0, :], 0.0)
            dve.drain().then_inc(setup.sem, 2)

            def tile_sum(w, g, to):
                dve.scalar_tensor_tensor(unused[:, :], w, 1.0, cond_bc[:, g, :], ALU.mult, ALU.mult, accum_out=to)
                dve.drain()

            def chunk_sums():
                for t in range(2):
                    for g in range(2):
                        tile_sum(ada_raw[:, t, :], g, ada_sum[:, t, g:g + 1])
                dve.sem_inc(ada_used.sem, 1)

            def add_bias(tile, count, src, bias_at):
                dve.tensor_tensor(mod[:, bass.ds(tile, count), :], src,
                                  ada_bt[:, bass.ds(bias_at, count), :].to_broadcast([P, count, 2]), ALU.add)

            dve.wait_ge(first_cond, 2)
            for n in range(PIECES_V):
                dve.wait_ge(first_landed[PIECES_T + n], 16)
                for g in range(2):
                    tile_sum(first_raw[:, PIECES_T + n, :], g, gates[:, 0, n, g:g + 1])
            add_bias(PIECES_T, PIECES_V, gates[:, 0, 0:PIECES_V, :], PIECES_T)
            dve.memset(sum_x, 0.0)
            dve.drain()
            for k in range(KT):
                dve.wait_ge(sq_ready.sem, k + 1)
                dve.tensor_tensor(sum_x, sum_x, sq2[:, k % 2, :], ALU.add).then_inc(sq_used.sem, 1)
                dve.drain()
            dve.drain().then_inc(sum_ready.sem, 1)
            dve.wait_ge(first_landed[-1], 16)
            chunk_sums()
            add_bias(PIECES_T + PIECES_V, 2, ada_sum[:, :, :], PIECES_T + PIECES_V)
            dve.wait_ge(hi_ready.sem, 1)
            dve.tensor_tensor(W_lo[0][:, :], raw[0][:, :], W_hi[0][:, :].bitcast(fp32),
                              ALU.subtract).then_inc(split_ready.sem, 1)
            dve.wait_ge(first_sum, 1)
            add_bias(0, PIECES_T, PS[:, 7, 0:2 * PIECES_T].rearrange("p (t g) -> p t g", g=2), 0)
            dve.drain()

            def add_squares(l, j, k, p):
                dve.wait_ge(sq_ready.sem, sq_ready.at(l, k + (j * KT + 1)))
                dve.tensor_tensor(sum_x, sum_x, sq2[:, p, :], ALU.add).then_inc(sq_used.sem, 1)
                dve.drain()

            def gates_of(j):
                dve.tensor_scalar(gates[:, j, :, :], mod[:, (3 * j + 2) * KT:(3 * j + 3) * KT, :],
                                  1.0 if j == 1 else 0.5, None, ALU.mult)

            def modulation(l, n, tile):
                dve.wait_ge(ada_landed.sem, ada_landed.at(l, 16 * n + 16))
                chunk_sums()
                add_bias(tile, 2, ada_sum[:, :, :], (l * N_ADA + n) * 2 + 2 * ADA_FIRST)

            def norm(l, j):
                g0 = PK["norm_g"][0]
                for g in range(2):
                    dve.scalar_tensor_tensor(up_by[:, j, :, g], mod[:, (3 * j + 1) * KT:(3 * j + 2) * KT, g], 1.0,
                                             par[:, g0 + j * KT:g0 + (j + 1) * KT], ALU.add, ALU.mult)
                if j == 1:
                    gates_of(1)
                dve.drain().then_inc(mod_ready.sem, 1)
                dve.wait_ge(rs_ready.sem, rs_ready.at(l, j + 1))
                for k in range(KT + 1):
                    if k < KT:
                        for g, (a, b) in enumerate(((0, LAT), (LAT, T))):
                            done = dve.scalar_tensor_tensor(norm_t[:, k, a:b], X[:, k, a:b], up_by[:, j, k, g:g + 1],
                                                            rsq[:, a:b], ALU.mult, ALU.mult)
                        done.then_inc(scaled.sem, 1)
                    if k >= 1:
                        q = k - 1
                        dve.wait_ge(h_hi.sem, h_hi.at(l, j * KT + q + 1))
                        for g, (a, b) in enumerate(((0, LAT), (LAT, T))):
                            done = dve.scalar_tensor_tensor(H_lo[:, q, a:b], norm_t[:, q, a:b],
                                                            mod[:, 3 * j * KT + q, g:g + 1],
                                                            H_hi[:, q, a:b].bitcast(fp32), ALU.add, ALU.subtract)
                        done.then_inc(h_lo.sem, 1)

            def add_to_x(r, k, bank):
                for j, a, b, g in GROUPS:
                    xs = X[:, bass.ds(k, 1), a:b].rearrange("p o n -> p (o n)")
                    done = dve.scalar_tensor_tensor(xs, PS[:, bank + j, a - HT * j:b - HT * j],
                                                    gates[:, r, bass.ds(k, 1), g:g + 1].rearrange("p o g -> p (o g)"),
                                                    xs, ALU.mult, ALU.add)
                return done

            def up_chunk(l, f, c, q, p, ada):
                split_lo(l, c + 1, 1 - p)
                if ada is not None:
                    modulation(l, *ada)
                dve.wait_ge(gate_ready.sem, gate_ready.at(l, q + (f * FT + 1)))
                dve.wait_ge(f_lo.sem, f_lo.at(l, q + (f * FT - 1)))
                dve.tensor_tensor(two(ffn_t[:, p, :]), two(silu_t[:, p, :]), halves(4 * p + 2),
                                  ALU.mult).then_inc(emptied.sem, 1)

            def ffn(l, f, c):
                up_chunk(l, f, c, 0, 0, None)
                if f == 1:
                    dve.wait_ge(cond_ready.sem, cond_ready.at(l, 1))
                n = ADA_COUNT[f, 0] + 1
                up_chunk(l, f, c + 1, 1, 1, (n, 2 * (ADA_FIRST + n)))
                for part, size in enumerate(FF_PARTS):
                    q0 = FF_PARTS[0] * part
                    for a, b, m in ADA_LOOPS[f, part]:
                        with dve.Fori(a, b) as i:
                            for p in range(2):
                                q = 2 * i + (q0 + p)
                                up_chunk(l, f, 2 * i + (c + p), q, p,
                                         None if m is None else (q + ADA_COUNT[f, part], 4 * i + 2 * (p + m)))
                    c += size
                    if part == 1:
                        dve.wait_ge(f_lo.sem, f_lo.at(l, (f + 1) * FT))
                        dve.memset(sum_x, 0.0)
                    else:
                        gates_of(2 * f)
                    dve.drain()
                    with dve.Fori(0, KT // 2) as i:
                        for p in range(2):
                            split_lo(l, 2 * i + (c + p + 1), 1 - p)
                            if (f, part) == (0, 0):
                                modulation(l, 2 * i + (ADA_DOWN + p), 4 * i + 2 * (ADA_FIRST + ADA_DOWN + p))
                            dve.wait_ge(chunk_done.sem, chunk_done.at(l, 2 * i + (c + p + 1)))
                            add_to_x(2 * f, 2 * i + p, 4 * p).then_inc(emptied.sem, 1)
                            if part == 1:
                                add_squares(l, 2 * f, 2 * i + p, p)
                            else:
                                dve.drain()
                    c += KT
                dve.drain().then_inc(sum_ready.sem, 1)

            def to_lo(l, src, t0, n):
                for k in range(n):
                    dve.wait_ge(mix_hi.sem, mix_hi.at(l, MIX_AT[t0] + k + 1))
                    dve.tensor_tensor(H_lo[:, t0 + k, :], src[:, k, :], H_hi[:, t0 + k, :].bitcast(fp32),
                                      ALU.subtract).then_inc(mix_lo.sem, 1)

            with dve.Fori(0, DEPTH) as l:
                dve.wait_ge(par_landed.sem, par_landed.at(l, 64))
                dve.tensor_copy(lb_l[:, 0:1, :], lbs[:, bass.ds(l, 1), :])
                dve.tensor_copy(lb_l[:, 1:2, :], rest[:, bass.ds(l, 1), :])
                qk = PK["qk_g"][0]
                dve.tensor_scalar(qk_g[0:D_QK, 0:1], par[0:D_QK, qk:qk + 1], float(D_QK) ** -0.5, None, ALU.mult)
                dve.tensor_copy(qk_g[0:D_QK, 1:2], par[0:D_QK, qk + 1:qk + 2])
                norm(l, 0)
                ffn(l, 0, AT_FFN[0])

                norm(l, 1)
                with dve.Fori(0, 4) as i:
                    for p in range(2):
                        split_lo(l, 2 * i + (AT_WIN + p + 1), 1 - p)
                split_lo(l, AT_WIN + 9, 1)
                split_lo(l, AT_WIN + 10, 0)

                for t in range(5):
                    dve.wait_ge(y_mm.sem, y_mm.at(l, t + 1))
                    dve.tensor_copy(Y[:, t, :], PS[:, t, :]).then_inc(y_ready.sem, 1)
                dve.wait_ge(frs_ready.sem, frs_ready.at(l, 1))
                for g in range(2):
                    dve.scalar_tensor_tensor(two(fmix[:, g, :]), halves(2 * g), col("fnet_g", g), two(frs[:, :]),
                                             ALU.mult, ALU.mult).then_inc(mixed.sem, 1)
                to_lo(l, fmix, 6, 2)

                dve.wait_ge(gates_ready.sem, gates_ready.at(l, 1))
                for n in range(4):
                    dve.tensor_scalar(KP[:, n // 2, n % 2, :], KP[:, n // 2, n % 2, :], lb_l[:, 1, n:n + 1], None, ALU.mult)
                dve.drain()
                dve.wait_ge(vt_mm.sem, vt_mm.at(l, 1))
                dve.tensor_tensor(Kc[0][:, :], KP[:, 0, :, :].rearrange("p a t -> p (a t)"),
                                  KP[:, 1, :, :].rearrange("p a t -> p (a t)"), ALU.add).then_inc(lev_ready.sem, 1)
                dve.wait_ge(gates_ready.sem, gates_ready.at(l, 2))
                for n in range(4):
                    dve.tensor_scalar(U[:, U_F + n, :], U[:, U_F + n, :], lb_l[:, 1, n:n + 1], lb_l[:, 0, n:n + 1],
                                      ALU.mult, ALU.add)
                dve.tensor_copy(merge(Kc[1], 1), flip(KP, 0, 1))
                dve.drain()
                for d in range(2):
                    dve.tensor_tensor(QP[:, d, :, :], U[:, U_Q:U_Q + 2, :], U[:, U_F + 2 * d:U_F + 2 * d + 2, :], ALU.mult)
                dve.drain().then_inc(lev_ready.sem, 1)

                decay = D_a
                dve.wait_ge(tables_landed.sem, tables_landed.at(l, 32))
                for li in range(1 + len(LEVELS)):
                    if li >= 1:
                        m = LEVELS[li - 1]
                        nb = 2 * T // m
                        dve.tensor_tensor(flip(KP, 0, m), flip(KP, 0, m), each(decay, 1, nb // 2, m), ALU.mult)
                        if li < len(LEVELS):
                            dve.drain()
                            dve.tensor_copy(merge(Kc[(li + 1) % 2], 2 * m), flip(KP, 0, 2 * m))
                        if m == LEVELS[-1]:
                            nxt = D64[:, :, :, :].rearrange("p d a c -> p d (a c)")
                        else:
                            nxt = (D_b if decay is D_a else D_a)[:, :, 0:nb // 2]
                        pairs = decay[:, :, 0:nb].rearrange("p d (n two) -> p d n two", two=2)
                        dve.tensor_tensor(nxt, pairs[:, :, :, 0], pairs[:, :, :, 1], ALU.mult)
                        for a in range(2):
                            dve.wait_ge(lev_mm.sem, lev_mm.at(l, 2 * li + a + 1))
                            dve.tensor_tensor(flip_pair(QP, 1, m, a), flip_pair(QP, 1, m, a),
                                              each(decay, 0, nb // 4, m, a * (nb // 2)), ALU.mult).then_inc(lev_ready.sem, 1)
                        dve.drain()
                        decay = D_b if decay is D_a else D_a
                    else:
                        dve.wait_ge(lev_mm.sem, lev_mm.at(l, 2))
                    scores = flat[:, 1536 * (li % 2):1536 * (li % 2) + 2 * T].rearrange("p (u t) -> p u t", t=C)
                    mask = masks[:, li:li + 1, :].to_broadcast([P, NU, C])
                    if li == 0:
                        dve.tensor_tensor(A[:, :, :], scores, mask, ALU.mult).then_inc(merged.sem, 1)
                    else:
                        dve.copy_predicated(A[:, :, :], mask.bitcast(u32), scores).then_inc(merged.sem, 1)
                    dve.drain()

                kv = flat[:, 0:2 * NU * C].rearrange("p (d a c v) -> p d a c v", d=2, a=2, c=NCH)
                dve.wait_ge(kv_mm.sem, kv_mm.at(l, 1))
                dve.wait_ge(s0_landed.sem, s0_landed.at(l, 32))

                def carry(d, a, frm, dst):
                    src = S[:, d, a, frm, :]
                    dve.scalar_tensor_tensor(dst, src, D64[:, d, a, frm:frm + 1], kv[:, d, a, frm, :], ALU.mult, ALU.add)

                last_c = NCH - 1
                for r in range(NC_LAT - 1):
                    for a in range(2):
                        carry(0, a, r, S[:, 0, a, r + 1, :])
                        carry(1, a, NC_LAT - 1 - r, S[:, 1, a, NC_LAT - 2 - r, :])
                        if r == 0:
                            dve.tensor_copy(S[:, 0, a, last_c, :], kv[:, 0, a, NC_LAT, :])
                            dve.tensor_copy(S[:, 1, a, NC_LAT, :], kv[:, 1, a, last_c, :])
                        if r == 1:
                            carry(0, a, last_c, fin_s[:, 0, a, :])
                            carry(1, a, NC_LAT, fin_s[:, 1, a, :])
                    dve.drain()
                dve.drain().then_inc(s_ready.sem, 1)
                dve.wait_ge(ck_hi_ready.sem, ck_hi_ready.at(l, 1))
                dve.tensor_tensor(ck_lo[:, :, 0:T], U[:, U_CKV:U_CKV + KVT, :], ck_hi[:, :, 0:T].bitcast(fp32), ALU.subtract)
                dve.tensor_tensor(ck_lo[:, :, T:KEYS], ckvc[:, :, :], ck_hi[:, :, T:KEYS].bitcast(fp32), ALU.subtract)
                for b in range(2):
                    dve.tensor_copy(kraw[64:96, b, 0:T], U[64:96, U_KR, :])
                    dve.tensor_copy(kraw[64:96, b, T:KEYS], krc[64:96, :])
                dve.drain().then_inc(ck_lo_ready.sem, 1)
                dve.wait_ge(hrs_ready.sem, hrs_ready.at(l, 1))
                dve.scalar_tensor_tensor(hmix[:, :, :].rearrange("p a t -> p (a t)"), flat[:, 5 * 512:5 * 512 + 2 * T],
                                         col("hgrn_g"), hrs[:, :], ALU.mult, ALU.mult)
                dve.drain()
                for a in range(2):
                    dve.tensor_tensor(hmix[:, a, :], hmix[:, a, :], U[:, U_GATE + a, :], ALU.mult).then_inc(mixed.sem, 1)
                to_lo(l, hmix, 0, 2)

                dve.wait_ge(stored.sem, stored.at(l, 32))
                dve.wait_ge(cq_lo_ready.sem, cq_lo_ready.at(l, 1))

                def copy_k(l, h):
                    if h:
                        dve.drain()
                    dve.wait_ge(heads["k", "proj"].sem, heads["k", "proj"].at(l, h + 1))
                    dve.tensor_copy(two(kraw[0:D_NOPE, h % 2, :], HK), halves(2 * (h % 2), HK, slice(0, D_NOPE)))\
                       .then_inc(heads["k", "copied"].sem, 1)

                def norm_head(l, kind, h):
                    dve.wait_ge(heads[kind, "rsqrt"].sem, heads[kind, "rsqrt"].at(l, h + 1))
                    if kind == "k":
                        out, src, rs = K_t[:, h, :], kraw[:, h % 2, :], krs[:, h % 2, :]
                    else:
                        out, src, rs = Q_t[:, h, :], qraw[:, h % 2, :], qrs[:, 0, :]
                    g = 1 if kind == "k" else 0
                    dve.scalar_tensor_tensor(out, src, qk_g[0:D_QK, g:g + 1], rs, ALU.mult, ALU.mult)\
                       .then_inc(heads[kind, "normed"].sem, 1)

                def turn_head(l, kind, h):
                    dst = (K_t if kind == "k" else Q_t)[64:96, h, 0:LAT]
                    tmp = PS[64:96, 6, :]
                    dve.wait_ge(heads[kind, "turned_mm"].sem, heads[kind, "turned_mm"].at(l, h + 1))
                    dve.tensor_tensor(tmp, tmp, sin, ALU.mult)
                    dve.tensor_tensor(dst, dst, cos, ALU.mult)
                    dve.drain()
                    dve.tensor_tensor(dst, dst, tmp, ALU.add).then_inc(heads[kind, "turned"].sem, 1)

                for h in range(H_MLA + 3):
                    if 2 <= h < H_MLA + 2:
                        norm_head(l, "k", h - 2)
                    if h < H_MLA:
                        copy_k(l, h)
                    if h >= 3:
                        turn_head(l, "k", h - 3)
                    if h >= H_MLA:
                        for t in range(2 * (h - H_MLA), 2 * (h - H_MLA) + 2):
                            dve.wait_ge(v_mm.sem, v_mm.at(l, t + 1))
                            dve.tensor_copy(V[:, t, :], PS[:, t % 4, :]).then_inc(v_ready.sem, 1)
                dve.drain().then_inc(emptied.sem, 1)
                split_lo(l, AT_WIN + 11, 1)
                for h in range(H_MLA + 3):
                    if 2 <= h < H_MLA + 2:
                        norm_head(l, "q", h - 2)
                    if h >= 3:
                        turn_head(l, "q", h - 3)
                    if h in (5, 9):
                        dve.drain().then_inc(emptied.sem, 1)
                    if h == 6:
                        split_lo(l, AT_OUT, 0)
                dve.drain().then_inc(q_ready.sem, 1)

                def row_max(l, u):
                    w = T if UNITS[u][1] < 4 else CTX
                    dve.wait_ge(sc_mm.sem, sc_mm.at(l, u + 1))
                    dve.tensor_reduce(nmax[:, u % 8:u % 8 + 1], flat[:, 1024 * (u % 2):1024 * (u % 2) + w], AX.X, ALU.max,
                                      negate=True).then_inc(max_ready.sem, 1)

                def scale_probs(l, u):
                    w = T if UNITS[u][1] < 4 else CTX
                    dve.wait_ge(exp_ready.sem, exp_ready.at(l, u + 1))
                    dve.reciprocal(rinv[:, u % 8:u % 8 + 1], rsum[:, u % 8:u % 8 + 1])
                    dve.drain()
                    dve.tensor_scalar(probs[:, u % 2, 0:w], probs[:, u % 2, 0:w], rinv[:, u % 8:u % 8 + 1], None,
                                      ALU.mult).then_inc(p_ready.sem, 1)

                def copy_om(l, u):
                    h, t = UNITS[u]
                    rows = slice(C * (h % 2), C * (h % 2) + C)
                    dve.wait_ge(pv_mm.sem, pv_mm.at(l, u + 1))
                    dve.tensor_copy(O_m[rows, h // 2, t * P:(t + 1) * P], PS[rows, 6 + u % 2, 0:P]).then_inc(om_ready.sem, 1)

                n = len(UNITS)
                for u in range(n + 2):
                    if 1 <= u <= n:
                        scale_probs(l, u - 1)
                    if u < n:
                        row_max(l, u)
                    if u >= 2:
                        copy_om(l, u - 2)
                dve.wait_ge(ors_ready.sem, ors_ready.at(l, 1))
                for k in range(4):
                    dve.scalar_tensor_tensor(O_m[:, k, :], O_m[:, k, :], col("mla_g", k), ors[:, :], ALU.mult,
                                             ALU.mult).then_inc(mixed.sem, 1)
                to_lo(l, O_m, 2, 4)
                dve.drain()
                dve.memset(sum_x, 0.0)
                dve.drain().then_inc(ada_used.sem, 1)
                with dve.Fori(0, N_OUT // 2) as i:
                    for p in range(2):
                        split_lo(l, 2 * i + (AT_OUT + p + 1), 1 - p)
                        dve.wait_ge(chunk_done.sem, chunk_done.at(l, 2 * i + (AT_OUT + p + 1)))
                        add_to_x(1, 4 * i + 2 * p, 4 * p)
                        add_to_x(1, 4 * i + (2 * p + 1), 4 * p + 2).then_inc(emptied.sem, 1)
                        for t in range(2):
                            add_squares(l, 1, 4 * i + (2 * p + t), t)
                dve.drain().then_inc(sum_ready.sem, 1)

                norm(l, 2)
                ffn(l, 1, AT_FFN[1])

        @block.tensor
        def _(pe):
            def mm(out, lhs, rhs, start, stop):
                return nc.tensor.matmul(out, lhs, rhs, start=start, stop=stop)

            def split_product(outs, lhs, rhs, kts, before=None):
                n = 3 * kts
                for j, out in enumerate(outs):
                    at_ = 0
                    for k in range(kts):
                        if before and j == 0 and k == before[0]:
                            pe.wait_ge(before[1], before[2])
                        (w1, w2), (h1, h2) = lhs(k), rhs(k, j)
                        for w, h in ((w1, h1), (w2, h1), (w1, h2)):
                            last = mm(out, w, h, at_ == 0, at_ == n - 1)
                            at_ += 1
                return last

            def hold():
                pe.sem_inc(wait_passed, 1)

            def begin(l, c):
                pe.wait_ge(split_ready.sem, split_ready.at(l, c + 1))
                pe.wait_ge(emptied.sem, emptied.at(l, c - 1))

            def weights(p, off, step=0):
                return lambda k: (W_hi[p][:, off + k * step:off + k * step + P], W_lo[p][:, off + k * step:off + k * step + P])

            def h_tile(k, j):
                return H_hi[:, k, j * HT:(j + 1) * HT], H_lo[:, k, j * HT:(j + 1) * HT]

            def f_tile(k, j):
                return F_hi[:, k, j * HT:(j + 1) * HT], F_lo[:, k, j * HT:(j + 1) * HT]

            def outs(bank, n=HT, rows=slice(0, P)):
                return [PS[rows, bank + j, 0:n] for j in range(2)]

            def two_tiles(p):
                split_product(outs(4 * p), weights(p, 0, 2 * P), h_tile, KT)
                return split_product(outs(4 * p + 2), weights(p, P, 2 * P), h_tile, KT)

            def sums(bank, stat, src, n=HT):
                for j in range(2):
                    for k, s in enumerate(src):
                        last = mm(PS[0:stat.shape[1], bank + j, 0:n], stat, s[:, j * n:(j + 1) * n], k == 0, k == len(src) - 1)
                return last

            def norm(l, j):
                pe.wait_ge(sum_ready.sem, sum_ready.at(l, j + 1))
                sums(0, ones, [sum_x]).then_inc(stat_mm.sem, 1)

            def abreast(k, start, stop):
                for n in range(4):
                    off = 2 * P * k + P * (n // 2)
                    w = W_hi[0][:, off:off + P], W_lo[0][:, off:off + P]
                    h = h_tile(k, n % 2)
                    for i, (x, y) in enumerate(((w[0], h[0]), (w[1], h[0]), (w[0], h[1]))):
                        last = mm(PS[:, n, 0:HT], x, y, start and i == 0, stop and i == 2)
                return last

            def first_chunk(l, j, c):
                begin(l, c)
                for k in range(KT):
                    pe.wait_ge(h_lo.sem, h_lo.at(l, j * KT + k + 1))
                    last = abreast(k, k == 0, k == KT - 1)
                last.then_inc(chunk_done.sem, 1)

            def ffn(l, f, c):
                done = 0
                first_chunk(l, 2 * f, c)
                begin(l, c + 1)
                two_tiles(1).then_inc(chunk_done.sem, 1)
                for n, part in enumerate(FF_PARTS):
                    with pe.Fori(1 - n, part // 2) as i:
                        for p in range(2):
                            begin(l, 2 * i + (c + p))
                            two_tiles(p).then_inc(chunk_done.sem, 1)
                    done += part
                    c += part
                    with pe.Fori(0, KT // 2) as i:
                        for p in range(2):
                            begin(l, 2 * i + (c + p))
                            pe.wait_ge(f_lo.sem, f_lo.at(l, f * FT + done - 2))
                            split_product(outs(4 * p), weights(p, 0, P), f_tile, part,
                                          before=(part - 2, f_lo.sem, f_lo.at(l, f * FT + done)))\
                                .then_inc(chunk_done.sem, 1)
                    c += KT

            pe.wait_ge(first_cond, 1)
            for n in range(PIECES_T):
                pe.wait_ge(first_landed[n], 16)
                for k in range(KT):
                    last = mm(PS[:, 7, 2 * n:2 * n + 2], first_raw[:, n, k * P:(k + 1) * P], cond_f[:, k, :],
                              k == 0, k == KT - 1)
            last.then_inc(first_sum, 1)
            pe.wait_ge(const_landed, 48)
            hold()
            with pe.Fori(0, DEPTH) as l:
                norm(l, 0)
                ffn(l, 0, AT_FFN[0])

                norm(l, 1)
                first_chunk(l, 1, AT_WIN)
                begin(l, AT_WIN + 1)
                two_tiles(1).then_inc(chunk_done.sem, 1)
                with pe.Fori(1, 4) as i:
                    for p in range(2):
                        begin(l, 2 * i + (AT_WIN + p))
                        two_tiles(p).then_inc(chunk_done.sem, 1)
                begin(l, AT_WIN + 8)
                two_tiles(0).then_inc(chunk_done.sem, 1)

                pe.wait_ge(emptied.sem, emptied.at(l, AT_WIN + 9))
                pe.wait_ge(par_landed.sem, par_landed.at(l, 64))
                for t in range(5):
                    for g in range(2):
                        last = mm(PS[:, t, 2 * P * g:2 * P * (g + 1)], U[:, U_FN + g, t * P:(t + 1) * P], chan, True, True)
                    last.then_inc(y_mm.sem, 1)
                pe.wait_ge(dft_landed.sem, dft_landed.at(l, 16))
                pe.wait_ge(y_ready.sem, y_ready.at(l, 5))
                for g in range(2):
                    for t in range(4):
                        for s in range(2):
                            o = (4 * s + t) * LAT
                            mm(PS[:, 5 + g, :], Y[:, t, 2 * P * g + P * s:2 * P * g + P * (s + 1)], dft_t[:, o:o + LAT],
                               t == 0 and s == 0, t == 3 and s == 1)
                    for s in range(2):
                        o = 8 * LAT + s * P
                        last = mm(PS[:, 7, g * P:(g + 1) * P], Y[:, 4, 2 * P * g + P * s:2 * P * g + P * (s + 1)],
                                  dft_t[:, o:o + P], s == 0, s == 1)
                    last.then_inc(spec_mm.sem, 1)
                    if g == 0:
                        pe.wait_ge(spec_ready.sem, spec_ready.at(l, 1))
                for g in range(2):
                    pe.wait_ge(spec_ready.sem, spec_ready.at(l, g + 1))
                    for j in range(2):
                        last = mm(PS[:, 2 * g + j, 0:HT], fw_t[:, g, :], spec[:, g, j * HT:(j + 1) * HT], True, True)
                    last.then_inc(fn_mm.sem, 1)
                pe.wait_ge(fsq_ready.sem, fsq_ready.at(l, 1))
                sums(4, ones, [fsq[:, g, :] for g in range(2)]).then_inc(fstat_mm.sem, 1)

                def turn_units(src, n):
                    hold()
                    for r, units in alternate(range(n)):
                        rows = slice(C * r, C * r + C)
                        for u in units:
                            last = mm(flat[rows, u * C:(u + 1) * C], src[rows, u * C:(u + 1) * C], ident[rows, rows],
                                      True, True)
                    return last

                pe.wait_ge(frs_ready.sem, frs_ready.at(l, 1))
                pe.wait_ge(csq_ready.sem, csq_ready.at(l, 1))
                sums(6, ones, [csq_q[:, k, :] for k in range(QT_)])
                sums(4, ones, [csq_kv[:, k, :] for k in range(KVT)]).then_inc(cstat_mm.sem, 1)
                pe.wait_ge(mixed.sem, mixed.at(l, 2))
                turn_units(U[:, U_V:U_V + 2, :].rearrange("p a t -> p (a t)"), NU).then_inc(vt_mm.sem, 1)
                pe.wait_ge(v_tok.sem, v_tok.at(l, 1))
                q_raw = U[:, U_Q:U_Q + 2, :].rearrange("p a t -> p (a t)")
                for li in range(1 + len(LEVELS)):
                    if li == 1:
                        pe.wait_ge(crs_ready.sem, crs_ready.at(l, 1))
                    if li >= 2:
                        pe.wait_ge(merged.sem, merged.at(l, li - 1))
                    for a in range(2):
                        pe.wait_ge(lev_ready.sem, lev_ready.at(l, 2 * li - 1 + a if li >= 2 else li + 1))
                        hold()
                        for r, units in alternate(range(a * NCH, (a + 1) * NCH)):
                            rows = slice(C * r, C * r + C)
                            for u in units:
                                if li == 0:
                                    keys, queries = Kc[0][rows, u * C:(u + 1) * C], q_raw[rows, u * C:(u + 1) * C]
                                else:
                                    m = LEVELS[li - 1]
                                    keys, queries = Kc[li % 2][rows, u * C:(u + 1) * C], pick(QP, m, u, rows)
                                o = 1536 * (li % 2) + u * C
                                last = mm(flat[rows, o:o + C], keys, queries, True, True)
                        last.then_inc(lev_mm.sem, 1)
                pe.wait_ge(lev_ready.sem, lev_ready.at(l, 2 + 2 * len(LEVELS)))
                pe.wait_ge(merged.sem, merged.at(l, 1 + len(LEVELS)))
                turn_units(KP[:, :, :, :].rearrange("p d a t -> p (d a t)"), 2 * NU).then_inc(kt_mm.sem, 1)
                pe.wait_ge(k_tok.sem, k_tok.at(l, 1))
                hold()
                for r, units in alternate(range(2 * NU)):
                    rows = slice(C * r, C * r + C)
                    for u in units:
                        last = mm(flat[rows, u * C:(u + 1) * C], Ktok[rows, u, :], Vtok[rows, u % NU, :], True, True)
                last.then_inc(kv_mm.sem, 1)
                def out_of(u, rows):
                    return flat[rows, 5 * 512 + u * C:5 * 512 + (u + 1) * C]

                for r, units in alternate(range(NU)):
                    rows = slice(C * r, C * r + C)
                    for u in units:
                        mm(out_of(u, rows), Vtok[rows, u, :], A[rows, u, :], u == units[0], False)
                pe.wait_ge(s_ready.sem, s_ready.at(l, 1))
                hold()
                for r, units in alternate(range(NU)):
                    rows = slice(C * r, C * r + C)
                    for u in units:
                        a, c = u // NCH, u % NCH
                        scans = [d for d in range(2) if c != (NC_LAT, NCH - 1)[d]]
                        for d in scans:
                            last = mm(out_of(u, rows), S[rows, d, a, c, :], QP[rows, d, a, c * C:(c + 1) * C],
                                      False, u == units[-1] and d == scans[-1])
                last.then_inc(o_mm.sem, 1)
                pe.wait_ge(hsq_ready.sem, hsq_ready.at(l, 1))
                for b in range(0, 2 * T, 512):
                    n = min(512, 2 * T - b)
                    last = mm(flat[:, b:b + n], pair_ones, hsq[:, b:b + n], True, True)
                last.then_inc(hstat_mm.sem, 1)

                def project(l, kind, h):
                    if h >= 2:
                        what = "copied" if kind == "k" else "squares"
                        pe.wait_ge(heads[kind, what].sem, heads[kind, what].at(l, h - 1))
                    if kind == "k":
                        last = split_product(outs(2 * (h % 2), HK), weights(1, P * h, H_MLA * P),
                                             lambda k, j: (ck_hi[:, k, j * HK:(j + 1) * HK], ck_lo[:, k, j * HK:(j + 1) * HK]),
                                             KVT)
                    else:
                        last = split_product(outs(2 * (h % 2)), weights(h // 4, P * (h % 4), 4 * P),
                                             lambda k, j: (cq_hi[:, k, j * HT:(j + 1) * HT], cq_lo[:, k, j * HT:(j + 1) * HT]),
                                             QT_)
                    last.then_inc(heads[kind, "proj"].sem, 1)

                def head_sums(l, kind, h):
                    pe.wait_ge(heads[kind, "squares"].sem, heads[kind, "squares"].at(l, h + 1))
                    if h >= 1:
                        pe.wait_ge(heads[kind, "rsqrt"].sem, heads[kind, "rsqrt"].at(l, h))
                    src, n = (ksq, HK) if kind == "k" else (qsq, HT)
                    sums(4, ones[0:D_QK, 0:D_QK], [src[:, h % 2, :]], n).then_inc(heads[kind, "sums"].sem, 1)

                def exchange(l, kind, h):
                    pe.wait_ge(heads[kind, "normed"].sem, heads[kind, "normed"].at(l, h + 1))
                    if h >= 1:
                        pe.wait_ge(heads[kind, "turned"].sem, heads[kind, "turned"].at(l, h))
                    src = K_t if kind == "k" else Q_t
                    mm(PS[:, 6, :], turn, src[:, h, 0:LAT], True, True).then_inc(heads[kind, "turned_mm"].sem, 1)

                v_w = [w[1][:, :].rearrange("p (k h x) -> p k h x", k=KVT, h=H_MLA)[:, :, :, D_NOPE:] for w in (W_hi, W_lo)]

                def value_rows(l, t):
                    if t >= 4:
                        pe.wait_ge(v_ready.sem, v_ready.at(l, t - 3))
                    split_product([PS[:, t % 4, :]], lambda k: (ck_hi[:, k, t * P:(t + 1) * P], ck_lo[:, k, t * P:(t + 1) * P]),
                                  lambda k, j: (v_w[0][:, k], v_w[1][:, k]), KVT).then_inc(v_mm.sem, 1)

                pe.wait_ge(hrs_ready.sem, hrs_ready.at(l, 1))
                pe.wait_ge(ck_lo_ready.sem, ck_lo_ready.at(l, 1))
                pe.wait_ge(tables_landed.sem, tables_landed.at(l, 32))
                pe.wait_ge(split_ready.sem, split_ready.at(l, AT_WIN + 10))
                for h in range(H_MLA + 3):
                    if h < H_MLA:
                        project(l, "k", h)
                    if h == 1:
                        pe.wait_ge(mixed.sem, mixed.at(l, 4))
                    if 1 <= h <= H_MLA:
                        head_sums(l, "k", h - 1)
                    if h >= 3:
                        exchange(l, "k", h - 3)
                    if h == H_MLA:
                        pe.wait_ge(heads["k", "copied"].sem, heads["k", "copied"].at(l, H_MLA))
                    if h >= H_MLA:
                        for t in range(2 * (h - H_MLA), 2 * (h - H_MLA) + 2):
                            value_rows(l, t)
                pe.drain().then_inc(chunk_done.sem, 1)
                def scores(l, u):
                    h, t = UNITS[u]
                    if u >= 2:
                        pe.wait_ge(exp_ready.sem, exp_ready.at(l, u - 1))
                    q, b = Q_t[:, h, t * P:(t + 1) * P], 2 * (u % 2)
                    if t < 4:
                        mm(PS[:, b, :], q, K_t[:, h, 0:LAT], True, True)
                        last = mm(PS[:, b + 1, 0:PAST], q, K_t[:, h, T:KEYS], True, True)
                    else:
                        last = mm(PS[:, b, 0:CTX], q, K_t[:, h, LAT:T], True, True)
                    last.then_inc(sc_mm.sem, 1)

                pe.wait_ge(emptied.sem, emptied.at(l, AT_WIN + 10))
                pe.wait_ge(split_ready.sem, split_ready.at(l, AT_WIN + 11))
                pe.wait_ge(cq_lo_ready.sem, cq_lo_ready.at(l, 1))
                for h in range(H_MLA + 3):
                    if h == 4:
                        pe.wait_ge(split_ready.sem, split_ready.at(l, AT_WIN + 12))
                    if h < H_MLA:
                        project(l, "q", h)
                    if 1 <= h <= H_MLA:
                        head_sums(l, "q", h - 1)
                    if h >= 3:
                        exchange(l, "q", h - 3)
                    if h > H_MLA:
                        scores(l, h - H_MLA - 1)
                    if h in (3, 7):
                        pe.drain().then_inc(chunk_done.sem, 1)
                pe.wait_ge(q_ready.sem, q_ready.at(l, 1))

                def turn_probs(l, u):
                    pe.wait_ge(p_ready.sem, p_ready.at(l, u + 1))
                    if u >= 1:
                        pe.wait_ge(pt_ready.sem, pt_ready.at(l, u))
                    for k in range(5 if UNITS[u][1] < 4 else 1):
                        last = nc.tensor.transpose(in_tiles[:, 16 + k, :], probs[:, u % 2, k * P:(k + 1) * P], ident)
                    last.then_inc(pt_mm.sem, 1)

                def attend(l, u):
                    h, t = UNITS[u]
                    pe.wait_ge(pt_ready.sem, pt_ready.at(l, u + 1))
                    if u >= 2:
                        pe.wait_ge(om_ready.sem, om_ready.at(l, u - 1))
                    tiles = (0, 1, 2, 3, 5) if t < 4 else (4,)
                    for k, vt in enumerate(tiles):
                        last = mm(PS[C * (h % 2):C * (h % 2) + C, 6 + u % 2, 0:P], V[:, vt, h * D_V:(h + 1) * D_V],
                                  probs_t[:, u % 2, k * P:(k + 1) * P], k == 0, k == len(tiles) - 1)
                    last.then_inc(pv_mm.sem, 1)

                n = len(UNITS)
                for u in range(n + 2):
                    if 2 <= u < n:
                        scores(l, u)
                    if 1 <= u <= n:
                        turn_probs(l, u - 1)
                    if u >= 2:
                        attend(l, u - 2)
                begin(l, AT_OUT)
                for n, k in enumerate((6, 7, 0, 1, 2, 3, 4, 5)):
                    if n == 2:
                        pe.wait_ge(osq_ready.sem, osq_ready.at(l, 1))
                        sums(4, ones, [osq[:, t, :] for t in range(4)]).then_inc(ostat_mm.sem, 1)
                    if n >= 4:
                        pe.wait_ge(mix_lo.sem, mix_lo.at(l, n + 1))
                    last = abreast(k, n == 0, n == KT - 1)
                last.then_inc(chunk_done.sem, 1)
                begin(l, AT_OUT + 1)
                two_tiles(1).then_inc(chunk_done.sem, 1)
                hold()
                with pe.Fori(1, N_OUT // 2) as i:
                    for p in range(2):
                        begin(l, 2 * i + (AT_OUT + p))
                        two_tiles(p).then_inc(chunk_done.sem, 1)

                norm(l, 2)
                ffn(l, 1, AT_FFN[1])


def rope_tables():
    n = D_ROPE // 4
    pos = np.stack([np.arange(LAT) // 64, np.arange(LAT) % 64]).astype(np.float32)
    freq = (np.float32(10000.0) ** (-np.arange(n, dtype=np.float32) / n)).astype(np.float32)
    ang = (pos[:, None, None, :] * freq[None, None, :, None]).astype(np.float32)
    ang = np.broadcast_to(ang, (2, 2, n, LAT)).reshape(D_ROPE, LAT)
    out = np.zeros((P, 2 * LAT + P), np.float32)
    turn = out[64:96, 2 * LAT + 64:2 * LAT + 96]
    for a in range(2):
        for f in range(n):
            x1, x2 = a * 2 * n + f, a * 2 * n + n + f
            turn[x2, x1] = -1.0
            turn[x1, x2] = 1.0
    out[64:96, 0:2 * LAT] = np.concatenate([np.cos(ang), np.sin(ang)], 1)
    return out


def fourier_tables():
    def table(n):
        a = 2 * np.pi * (np.outer(np.arange(n), np.arange(n)) % n) / n
        s = 1 / np.sqrt(n * 64.0)
        return np.cos(a) * s, -np.sin(a) * s
    c, s = (m.reshape(4, P, LAT).transpose(1, 0, 2).reshape(P, 4 * LAT) for m in table(LAT))
    cc, ss = table(CTX)
    return np.ascontiguousarray(np.concatenate([c, s, cc, ss], 1).astype(np.float32))


def const_tables():
    pair = np.kron(np.eye(2), np.ones((C, C)))
    s, t = np.arange(P)[:, None] % C, np.arange(C)[None, :]
    masks = [(s == t)] + [(s // (2 * m) == t // (2 * m)) & (s // m != t // m) for m in LEVELS]
    a = 2 * np.pi * (np.outer(np.arange(64), np.arange(64)) % 64) / 64
    chan = [np.kron(np.eye(2), f(a)) for f in (np.cos, np.sin)]
    return (np.concatenate([np.ones((P, P)), pair, np.eye(P), *chan], 1).astype(np.float32),
            np.stack(masks, 1).astype(np.float32))


_OUTS = [("yT", (P, KT, T)), ("ckv_out", (DEPTH, P, KVT, CTX)), ("kr_out", (DEPTH, D_ROPE, CTX)),
         ("state_out", (DEPTH, P, 2, 2, C))]


def kernel(x_prompt, x_sample, cache_ckv, cache_krope, state_hgrn, c, c_ctx, ada_w, ada_b, norm_g, ffn_w_gu,
           ffn_w_down, w_in, hgrn_lb, hgrn_norm_g, mla_q_norm_g, mla_w_q_up, mla_kv_norm_g, mla_w_kv_up,
           mla_qk_norm_g, mla_out_norm_g, fnet_w, fnet_norm_g, w_out):
    import numpy as np
    import concourse.bacc as bacc
    from concourse import mybir as _mybir
    from concourse.bass_utils import run_bass_kernel_spmd

    f = np.float32
    L = DEPTH
    def tiles(a, *lead):
        return np.swapaxes(a.reshape(*a.shape[:-1], -1, P), -1, -2)

    x = np.concatenate([x_sample[0], x_prompt[0]], 0)
    ins = {}
    ins["xT"] = x.reshape(T, KT, P).transpose(2, 1, 0)
    ins["condT"] = np.stack([c[0], c_ctx], -1).reshape(KT, P, 2).transpose(1, 0, 2)
    ada = ada_w.reshape(L, D_MODEL, N_ADA, 2, P).transpose(0, 2, 4, 3, 1).reshape(L * N_ADA, P, CHUNK)
    ins["ada_p"] = np.concatenate([ada[ADA_FIRST - 1:], np.zeros((ADA_FIRST, P, CHUNK), f)], 0)
    ins["cond_b"] = np.broadcast_to(np.stack([c[0], c_ctx])[None], (P, 2, D_MODEL))
    first = ada_w[0, :, :PIECES_T * P].reshape(KT, P, PIECES_T, P)
    ins["ada_first"] = first.transpose(2, 1, 0, 3).reshape(PIECES_T, P, D_MODEL)
    ins["ada_second"] = ada_w[0, :, PIECES_T * P:(PIECES_T + PIECES_V) * P].T.reshape(PIECES_V, P, D_MODEL)
    bias = np.concatenate([*tiles(ada_b), np.zeros((P, 2 * ADA_FIRST), f)], -1)
    ins["ada_b"] = bias[:, :, None]
    pk = [np.concatenate([tiles(norm_g[:, i]) for i in range(3)], -1),
          np.concatenate([hgrn_norm_g, hgrn_norm_g], 1)[:, :, None], tiles(mla_q_norm_g), tiles(mla_kv_norm_g),
          np.concatenate([mla_qk_norm_g.transpose(0, 2, 1), np.zeros((L, P - D_QK, 2), f)], 1),
          tiles(mla_out_norm_g), tiles(fnet_norm_g)]
    ins["params"] = np.concatenate(pk, -1)
    ins["lb"] = hgrn_lb.reshape(L, 2, 2, P).transpose(3, 0, 1, 2).reshape(P, L, 4)
    gu = ffn_w_gu.reshape(L * 2, KT, P, 2, FT, P).transpose(0, 4, 2, 1, 3, 5)
    ins["gu_p"] = np.concatenate([gu.reshape(L * 2 * FT, P, CHUNK), np.zeros((2, P, CHUNK), f)], 0)
    dn = ffn_w_down.reshape(L * 2, FT, P, KT, P)
    a = FF_PARTS[0]
    for name, part in (("down_a", dn[:, :a]), ("down_b", dn[:, a:])):
        ins[name] = part.transpose(0, 3, 2, 1, 4).reshape(L * 2 * KT, P, -1)
    z = lambda n: np.zeros((L, D_MODEL, n), f)
    cols = np.concatenate([w_in[:, :, :1920], z(64), w_in[:, :, 1920:1952], z(32), w_in[:, :, 1952:]], -1)
    ins["win_p"] = cols.reshape(L, KT, P, N_WIN, 256).transpose(0, 3, 2, 1, 4).reshape(L * N_WIN, P, CHUNK)
    ins["kv_p"] = mla_w_kv_up.reshape(L, KVT, P, 1024).transpose(0, 2, 1, 3).reshape(L, P, CHUNK)
    q = mla_w_q_up.reshape(L, QT_, P, 2, 4, D_QK)
    q = np.concatenate([q, np.zeros((L, QT_, P, 2, 4, P - D_QK), f)], -1)
    ins["q_p"] = q.transpose(0, 3, 2, 1, 4, 5).reshape(L * 2, P, QT_ * 4 * P)
    ins["out_p"] = w_out.reshape(L, KT, P, N_OUT, 256).transpose(0, 3, 2, 1, 4).reshape(L * N_OUT, P, CHUNK)
    fw = np.zeros((L, P, 2, P), f)
    for g in range(4):
        r = slice(64 * (g % 2), 64 * (g % 2) + 64)
        fw[:, r, g // 2, r] = fnet_w[:, g]
    ins["fnet_w"] = fw
    ins["ckvT"] = cache_ckv[0].transpose(0, 2, 1).reshape(L, KVT, P, PAST).transpose(0, 2, 1, 3)
    ins["kropeT"] = cache_krope[0].transpose(0, 2, 1)
    ins["state"] = state_hgrn[0].reshape(L, 2, 2, 2 * 64, 64).transpose(0, 3, 1, 2, 4)
    ins["consts"], ins["level_masks"] = const_tables()
    ins["dft"], ins["rope"] = fourier_tables(), rope_tables()

    nc = bacc.Bacc("TRN2", target_bir_lowering=False, num_devices=1)
    arrays, args = {}, []
    for name in ("xT", "condT", "cond_b", "ada_p", "ada_first", "ada_second", "ada_b", "params", "lb", "gu_p", "down_a",
                 "down_b", "win_p", "kv_p", "q_p", "out_p", "fnet_w", "ckvT", "kropeT", "state", "dft", "consts",
                 "level_masks", "rope"):
        arr = np.ascontiguousarray(ins[name])
        arrays[f"in_{name}"] = arr
        args.append(nc.dram_tensor(f"in_{name}", arr.shape, _mybir.dt.from_np(arr.dtype), kind="ExternalInput").ap())
    for name, shape in _OUTS:
        args.append(nc.dram_tensor(f"out_{name}", shape, _mybir.dt.float32, kind="ExternalOutput").ap())
    build(nc, *args)
    r = run_bass_kernel_spmd(nc, [arrays], core_ids=[0]).results[0]
    y = np.asarray(r["out_yT"]).transpose(2, 1, 0).reshape(T, D_MODEL)
    ckv = np.asarray(r["out_ckv_out"]).transpose(0, 3, 2, 1).reshape(1, L, CTX, KV_RANK)
    kr = np.asarray(r["out_kr_out"]).transpose(0, 2, 1).reshape(1, L, CTX, D_ROPE)
    st = np.asarray(r["out_state_out"]).transpose(0, 2, 3, 1, 4).reshape(1, L, 2, 4, 64, 64)
    return (np.ascontiguousarray(y[None, LAT:]), np.ascontiguousarray(y[None, :LAT]), np.ascontiguousarray(ckv),
            np.ascontiguousarray(kr), np.ascontiguousarray(st))
```
